# Optimizing a Trainium2 kernel written in Bass

```python
import math
import jax, jax.numpy as jnp
from jax import lax
import numpy as np

D_MODEL = 1024
BATCH = 1
SEQ = 512
DEPTH = 1

HEAD_DIM = 64
POOL_WIDTH = D_MODEL // 4
POOL_WINDOWS = (2, 4, 8, 16)
POOL_GROUPS = len(POOL_WINDOWS)
POOL_GROUP_DIM = POOL_WIDTH // POOL_GROUPS
ATTN_WIDTH = D_MODEL - POOL_WIDTH
ATTN_HEADS = ATTN_WIDTH // HEAD_DIM
DILATION_CFG = ((128, 1), (512, 4), (2048, 16))
N_DIL = len(DILATION_CFG)
HEADS_PER_DIL = ATTN_HEADS // N_DIL
ATTN_OUT_WIDTH = HEADS_PER_DIL * HEAD_DIM
IN_PROJ_WIDTH = POOL_WIDTH + 3 * ATTN_WIDTH
OUT_PROJ_WIDTH = POOL_WIDTH + ATTN_OUT_WIDTH
ROT_DIM = HEAD_DIM // 4
ROPE_THETA = 500000.0
D_FF = 11 * D_MODEL // 4
CONV_WIDTH = 3
BLOCK = 128
NORM_EPS = 1e-6
N_MOD = 6


def rms_norm(x, g):
    x32 = x.astype(jnp.float32)
    y = x32 * lax.rsqrt(jnp.mean(x32 * x32, axis=-1, keepdims=True) + NORM_EPS)
    return (y * g.astype(jnp.float32)).astype(x.dtype)

def partial_rope(t, cos, sin):
    half = ROT_DIM // 2
    t1 = t[..., :half]
    t2 = t[..., half:ROT_DIM]
    return jnp.concatenate(
        [t1 * cos - t2 * sin, t2 * cos + t1 * sin, t[..., ROT_DIM:]], axis=-1)

def causal_multiscale_pool(u, w_pool, b_pool, pool_scale):
    B, S, _ = u.shape
    u32 = u.astype(jnp.float32).reshape(B, S, POOL_GROUPS, POOL_GROUP_DIM)
    cs = jnp.cumsum(u32, axis=1)
    t = jnp.arange(S, dtype=jnp.float32)
    means = []
    for gi, w in enumerate(POOL_WINDOWS):
        csg = cs[:, :, gi]
        lagged = jnp.pad(csg[:, :S - w], ((0, 0), (w, 0), (0, 0)))
        count = jnp.minimum(t + 1.0, float(w))
        means.append((csg - lagged) / count[None, :, None])
    mixed = jnp.stack(means, axis=2) - u32
    y = jnp.einsum('bsgc,gcd->bsgd', mixed, w_pool.astype(jnp.float32)) + b_pool.astype(jnp.float32)
    return (y.reshape(B, S, POOL_WIDTH) * pool_scale.astype(jnp.float32)).astype(u.dtype)

def dilated_window_attention(q, k, v, window, dilation):
    B, S, H, hd = q.shape
    span = window // dilation
    assert span <= BLOCK
    chunk = dilation * BLOCK
    s_pad = -(-S // chunk) * chunk
    padw = ((0, 0), (0, s_pad - S), (0, 0), (0, 0))
    q, k, v = (jnp.pad(a.astype(jnp.float32), padw) for a in (q, k, v))
    nb = s_pad // chunk
    qb, kb, vb = (a.reshape(B, nb, BLOCK, dilation, H, hd) for a in (q, k, v))

    def with_prev(a):
        prev = jnp.pad(a[:, :-1], ((0, 0), (1, 0), (0, 0), (0, 0), (0, 0), (0, 0)))
        return jnp.concatenate([prev, a], axis=2)

    kk, vv = with_prev(kb), with_prev(vb)
    scores = jnp.einsum('bnirhd,bnjrhd->bnrhij', qb, kk)
    i = jnp.arange(BLOCK)[:, None]
    j = jnp.arange(2 * BLOCK)[None, :]
    n = jnp.arange(nb)[:, None, None]
    dist = BLOCK + i - j
    valid = (dist >= 0) & (dist <= span) & (n * BLOCK + j - BLOCK >= 0)
    scores = jnp.where(valid[None, :, None, None], scores, -jnp.inf)
    m = jnp.max(scores, axis=-1, keepdims=True)
    p = jnp.exp(scores - m)
    den = jnp.sum(p, axis=-1)
    o = jnp.einsum('bnrhij,bnjrhd->bnirhd', p, vv)
    den_t = jnp.moveaxis(den, -1, 2)
    lse_t = jnp.moveaxis(m[..., 0] + jnp.log(den), -1, 2)
    o = (o / den_t[..., None]).reshape(B, s_pad, H, hd)[:, :S]
    lse = lse_t.reshape(B, s_pad, H)[:, :S]
    return o, lse

def mixing_sublayer(h, cos, sin, w_in, w_pool, b_pool, pool_scale, w_out):
    B, S, _ = h.shape
    proj = h @ w_in
    u_pool = proj[..., :POOL_WIDTH]
    qkv = proj[..., POOL_WIDTH:].reshape(B, S, 3, ATTN_HEADS, HEAD_DIM)
    q = partial_rope(qkv[:, :, 0], cos, sin) * (HEAD_DIM ** -0.5)
    k = partial_rope(qkv[:, :, 1], cos, sin)
    v = qkv[:, :, 2]
    outs, lses = [], []
    for g, (window, dilation) in enumerate(DILATION_CFG):
        sl = slice(g * HEADS_PER_DIL, (g + 1) * HEADS_PER_DIL)
        o, l = dilated_window_attention(q[:, :, sl], k[:, :, sl], v[:, :, sl], window, dilation)
        outs.append(o)
        lses.append(l)
    alpha = jax.nn.softmax(jnp.stack(lses, axis=0), axis=0)
    attn = jnp.sum(alpha[..., None] * jnp.stack(outs, axis=0), axis=0)
    attn = attn.reshape(B, S, ATTN_OUT_WIDTH).astype(h.dtype)
    pool = causal_multiscale_pool(u_pool, w_pool, b_pool, pool_scale)
    return jnp.concatenate([pool, attn], axis=-1) @ w_out

def conv_ffn(h, w_up, conv_w, conv_b, w_down):
    S = h.shape[1]
    up = h @ w_up
    gate, val = up[..., :D_FF], up[..., D_FF:]
    gp = jnp.pad(gate, ((0, 0), (CONV_WIDTH - 1, 0), (0, 0)))
    gate = gp[:, 0:S] * conv_w[0] + gp[:, 1:S + 1] * conv_w[1] + gp[:, 2:S + 2] * conv_w[2] + conv_b
    return (jax.nn.gelu(gate, approximate=True) * val) @ w_down

def first_inputs(seed: int = 0) -> dict:
    key = jax.random.key(seed)
    ks = jax.random.split(key, 20)
    f32 = jnp.float32
    nrm = lambda k, shape, s: jax.random.normal(k, shape, f32) * s
    L = DEPTH
    return {
        "x": nrm(ks[0], (BATCH, SEQ, D_MODEL), 1.0),
        "c": nrm(ks[1], (BATCH, D_MODEL), 1.0),
        "positions": jnp.broadcast_to(jnp.arange(SEQ, dtype=jnp.int32), (BATCH, SEQ)),
        "w_ada": nrm(ks[2], (L, D_MODEL, N_MOD * D_MODEL), D_MODEL ** -0.5),
        "b_ada": nrm(ks[3], (L, N_MOD * D_MODEL), 0.02),
        "g_pre_mix": 1.0 + nrm(ks[4], (L, D_MODEL), 0.05),
        "g_post_mix": 1.0 + nrm(ks[5], (L, D_MODEL), 0.05),
        "g_pre_ffn": 1.0 + nrm(ks[6], (L, D_MODEL), 0.05),
        "g_post_ffn": 1.0 + nrm(ks[7], (L, D_MODEL), 0.05),
        "w_in": nrm(ks[8], (L, D_MODEL, IN_PROJ_WIDTH), D_MODEL ** -0.5),
        "w_pool": nrm(ks[9], (L, POOL_GROUPS, POOL_GROUP_DIM, POOL_GROUP_DIM), POOL_GROUP_DIM ** -0.5),
        "b_pool": nrm(ks[10], (L, POOL_GROUPS, POOL_GROUP_DIM), 0.02),
        "pool_scale": 1.0 + nrm(ks[11], (L, POOL_WIDTH), 0.05),
        "w_out": nrm(ks[12], (L, OUT_PROJ_WIDTH, D_MODEL), OUT_PROJ_WIDTH ** -0.5),
        "w_up": nrm(ks[13], (L, D_MODEL, 2 * D_FF), D_MODEL ** -0.5),
        "conv_w": nrm(ks[14], (L, CONV_WIDTH, D_FF), CONV_WIDTH ** -0.5),
        "conv_b": nrm(ks[15], (L, D_FF), 0.02),
        "w_down": nrm(ks[16], (L, D_FF, D_MODEL), D_FF ** -0.5),
    }

def first_block(x, c, positions, w_ada, b_ada, g_pre_mix, g_post_mix, g_pre_ffn, g_post_ffn,
              w_in, w_pool, b_pool, pool_scale, w_out, w_up, conv_w, conv_b, w_down):
    inv_freq = ROPE_THETA ** (-jnp.arange(0, ROT_DIM, 2, dtype=jnp.float32) / ROT_DIM)
    ang = positions.astype(jnp.float32)[..., None] * inv_freq
    cos = jnp.cos(ang)[:, :, None, :].astype(x.dtype)
    sin = jnp.sin(ang)[:, :, None, :].astype(x.dtype)
    c_act = jax.nn.silu(c)
    for l in range(DEPTH):
        mod = c_act @ w_ada[l] + b_ada[l]
        sh_m, sc_m, gt_m, sh_f, sc_f, gt_f = (t[:, None, :] for t in jnp.split(mod, N_MOD, axis=-1))
        h = rms_norm(x, g_pre_mix[l]) * (1.0 + sc_m) + sh_m
        y = mixing_sublayer(h, cos, sin, w_in[l], w_pool[l], b_pool[l], pool_scale[l], w_out[l])
        x = x + gt_m * rms_norm(y, g_post_mix[l])
        h = rms_norm(x, g_pre_ffn[l]) * (1.0 + sc_f) + sh_f
        y = conv_ffn(h, w_up[l], conv_w[l], conv_b[l], w_down[l])
        x = x + gt_f * rms_norm(y, g_post_ffn[l])
    return x


MEM_LEN = 256
CONV_W = 512
ATT_HEADS = 8
ATT_DH = 64
ATT_W = ATT_HEADS * ATT_DH
MOBA_BLOCK = 256
MOBA_TOPK = 3
Q_CHUNK = 16
MEM_HEADS = 4
MEM_DH = 128
MEM_W = MEM_HEADS * MEM_DH
NUM_BUCKETS = 32
MAX_EXACT = NUM_BUCKETS // 2
MAX_DISTANCE = 1024
D_FF_2 = 2816
FFN_CONV_WIDTH = 3
N_BRANCHES = 3
RMS_EPS = 1e-6
NEG = -1e30

IN_SPLITS = [CONV_W, CONV_W, CONV_W, ATT_W, ATT_W, ATT_W, MEM_W, D_MODEL, D_MODEL, D_MODEL]
IN_COLS = sum(IN_SPLITS)
IN_OFFSETS = list(np.cumsum(IN_SPLITS)[:-1])


def rmsnorm(x, g):
    x32 = x.astype(jnp.float32)
    y = x32 * lax.rsqrt(jnp.mean(x32 * x32, axis=-1, keepdims=True) + RMS_EPS)
    return (y * g.astype(jnp.float32)).astype(x.dtype)

def causal_dwconv(u, w, b=None):
    width, c = w.shape
    y = lax.conv_general_dilated(
        u, w.astype(u.dtype)[:, None, :], window_strides=(1,), padding=[(width - 1, 0)],
        dimension_numbers=("NWC", "WIO", "NWC"), feature_group_count=c)
    if b is not None:
        y = y + b.astype(u.dtype)
    return y

def rel_bucket(dist):
    n = jnp.maximum(dist, 0)
    is_small = n < MAX_EXACT
    n_f = jnp.maximum(n, MAX_EXACT).astype(jnp.float32)
    large = MAX_EXACT + (jnp.log(n_f / MAX_EXACT) / math.log(MAX_DISTANCE / MAX_EXACT)
                         * (NUM_BUCKETS - MAX_EXACT)).astype(jnp.int32)
    large = jnp.minimum(large, NUM_BUCKETS - 1)
    return jnp.where(is_small, n, large)

def moba_attention(q, k, v, rel_bias):
    b_, h_, s_, dh = q.shape
    nb = -(-s_ // MOBA_BLOCK)
    pad = nb * MOBA_BLOCK - s_
    k_pad = jnp.pad(k, ((0, 0), (0, 0), (0, pad), (0, 0)))
    v_pad = jnp.pad(v, ((0, 0), (0, 0), (0, pad), (0, 0)))
    kb = k_pad.reshape(b_, h_, nb, MOBA_BLOCK, dh)
    vb = v_pad.reshape(b_, h_, nb, MOBA_BLOCK, dh)
    scale = dh ** -0.5

    k_mean = jnp.mean(kb.astype(jnp.float32), axis=3)
    gate = jnp.einsum("bhsd,bhnd->bhsn", q.astype(jnp.float32), k_mean)
    q_blk = jnp.arange(s_) // MOBA_BLOCK
    past = jnp.arange(nb)[None, :] < q_blk[:, None]
    gate = jnp.where(past, gate, NEG)
    k_sel = max(1, min(MOBA_TOPK, nb - 1))
    _, sel = lax.top_k(gate, k_sel)

    bias_hb = rel_bias.astype(jnp.float32).T
    b_idx = jnp.arange(b_)[:, None, None, None]
    h_idx = jnp.arange(h_)[None, :, None, None]
    blk_off = jnp.arange(MOBA_BLOCK)

    def chunk(c):
        start = c * Q_CHUNK
        qc = lax.dynamic_slice_in_dim(q, start, Q_CHUNK, axis=2)
        selc = lax.dynamic_slice_in_dim(sel, start, Q_CHUNK, axis=2)
        t = start + jnp.arange(Q_CHUNK)
        valid = jnp.arange(k_sel)[None, :] < (t // MOBA_BLOCK)[:, None]
        kg = kb[b_idx, h_idx, selc]
        vg = vb[b_idx, h_idx, selc]
        s_sel = jnp.einsum("bhqd,bhqjkd->bhqjk", qc, kg).astype(jnp.float32) * scale
        k_pos = selc[..., None] * MOBA_BLOCK + blk_off
        bucket = rel_bucket(t[None, None, :, None, None] - k_pos)
        bias = bias_hb[h_idx[..., None], bucket]
        s_sel = jnp.where(valid[None, None, :, :, None], s_sel + bias, NEG)
        own = start // MOBA_BLOCK
        ko = lax.dynamic_slice_in_dim(k_pad, own * MOBA_BLOCK, MOBA_BLOCK, axis=2)
        vo = lax.dynamic_slice_in_dim(v_pad, own * MOBA_BLOCK, MOBA_BLOCK, axis=2)
        s_own = jnp.einsum("bhqd,bhkd->bhqk", qc, ko).astype(jnp.float32) * scale
        dist = t[:, None] - (own * MOBA_BLOCK + blk_off)[None, :]
        bias_own = bias_hb[:, rel_bucket(dist)]
        s_own = jnp.where(dist[None, None] >= 0, s_own + bias_own[None], NEG)
        logits = jnp.concatenate([s_sel.reshape(b_, h_, Q_CHUNK, k_sel * MOBA_BLOCK), s_own], axis=-1)
        p = jax.nn.softmax(logits, axis=-1).astype(v.dtype)
        p_sel = p[..., : k_sel * MOBA_BLOCK].reshape(b_, h_, Q_CHUNK, k_sel, MOBA_BLOCK)
        p_own = p[..., k_sel * MOBA_BLOCK:]
        return (jnp.einsum("bhqjk,bhqjkd->bhqd", p_sel, vg)
                + jnp.einsum("bhqk,bhkd->bhqd", p_own, vo))

    out = lax.map(chunk, jnp.arange(s_ // Q_CHUNK))
    return jnp.transpose(out, (1, 2, 0, 3, 4)).reshape(b_, h_, s_, dh)

def memory_attention(qm, mem_n, w_mem_kv):
    b_, s_, _ = qm.shape
    kv = mem_n @ w_mem_kv
    mk, mv = jnp.split(kv, 2, axis=-1)
    mk = mk.reshape(b_, -1, MEM_HEADS, MEM_DH)
    mv = mv.reshape(b_, -1, MEM_HEADS, MEM_DH)
    q4 = qm.reshape(b_, s_, MEM_HEADS, MEM_DH)
    s = jnp.einsum("bshd,bmhd->bhsm", q4, mk).astype(jnp.float32) * (MEM_DH ** -0.5)
    p = jax.nn.softmax(s, axis=-1).astype(qm.dtype)
    return jnp.einsum("bhsm,bmhd->bshd", p, mv).reshape(b_, s_, MEM_W)

def second_inputs(seed: int = 0) -> dict:
    key = jax.random.key(seed)
    ks = jax.random.split(key, 20)

    def nrm(k, shape, scale):
        return jax.random.normal(k, shape, jnp.float32) * scale

    def gain(k):
        return 1.0 + nrm(k, (DEPTH, D_MODEL), 0.05)

    return {
        "x": nrm(ks[0], (BATCH, SEQ, D_MODEL), 1.0),
        "mem": nrm(ks[1], (BATCH, MEM_LEN, D_MODEL), 1.0),
        "rel_bias": nrm(ks[2], (NUM_BUCKETS, ATT_HEADS), 0.5),
        "g_pre_mix": gain(ks[3]),
        "g_post_mix": gain(ks[4]),
        "g_pre_ffn": gain(ks[5]),
        "g_post_ffn": gain(ks[6]),
        "g_mem": gain(ks[7]),
        "w_in": nrm(ks[8], (DEPTH, D_MODEL, IN_COLS), D_MODEL ** -0.5),
        "b_gate": nrm(ks[9], (DEPTH, N_BRANCHES * D_MODEL), 0.01),
        "conv_mix_w": nrm(ks[10], (DEPTH, CONV_WIDTH, CONV_W), CONV_WIDTH ** -0.5),
        "w_conv_out": nrm(ks[11], (DEPTH, CONV_W, D_MODEL), CONV_W ** -0.5),
        "w_attn_out": nrm(ks[12], (DEPTH, ATT_W, D_MODEL), ATT_W ** -0.5),
        "w_mem_kv": nrm(ks[13], (DEPTH, D_MODEL, 2 * MEM_W), D_MODEL ** -0.5),
        "w_mem_out": nrm(ks[14], (DEPTH, MEM_W, D_MODEL), MEM_W ** -0.5),
        "w_out": nrm(ks[15], (DEPTH, D_MODEL, D_MODEL), D_MODEL ** -0.5),
        "w_up": nrm(ks[16], (DEPTH, D_MODEL, 2 * D_FF_2), D_MODEL ** -0.5),
        "ffn_conv_w": nrm(ks[17], (DEPTH, FFN_CONV_WIDTH, 2 * D_FF_2), FFN_CONV_WIDTH ** -0.5),
        "ffn_conv_b": nrm(ks[18], (DEPTH, 2 * D_FF_2), 0.01),
        "w_down": nrm(ks[19], (DEPTH, D_FF_2, D_MODEL), D_FF_2 ** -0.5),
    }

def second_block(x, mem, rel_bias, g_pre_mix, g_post_mix, g_pre_ffn, g_post_ffn, g_mem,
              w_in, b_gate, conv_mix_w, w_conv_out, w_attn_out, w_mem_kv, w_mem_out,
              w_out, w_up, ffn_conv_w, ffn_conv_b, w_down):
    b_, s_, d_ = x.shape
    for l in range(DEPTH):
        h = rmsnorm(x, g_pre_mix[l])
        proj = h @ w_in[l]
        (cb, cc, cv, q, k, v, qm, ga, gb, gc) = jnp.split(proj, IN_OFFSETS, axis=-1)
        y_a = (cb * causal_dwconv(cc * cv, conv_mix_w[l])) @ w_conv_out[l]
        to_heads = lambda t: jnp.transpose(t.reshape(b_, s_, ATT_HEADS, ATT_DH), (0, 2, 1, 3))
        o = moba_attention(to_heads(q), to_heads(k), to_heads(v), rel_bias)
        y_b = jnp.transpose(o, (0, 2, 1, 3)).reshape(b_, s_, ATT_W) @ w_attn_out[l]
        y_c = memory_attention(qm, rmsnorm(mem, g_mem[l]), w_mem_kv[l]) @ w_mem_out[l]
        bg = b_gate[l].reshape(N_BRANCHES, d_)
        merged = (jax.nn.sigmoid(ga + bg[0]) * y_a + jax.nn.sigmoid(gb + bg[1]) * y_b
                  + jax.nn.sigmoid(gc + bg[2]) * y_c)
        x = x + rmsnorm(merged @ w_out[l], g_post_mix[l])
        h = rmsnorm(x, g_pre_ffn[l])
        u = causal_dwconv(h @ w_up[l], ffn_conv_w[l], ffn_conv_b[l])
        a, g = jnp.split(u, 2, axis=-1)
        f = (jax.nn.gelu(a) * g) @ w_down[l]
        x = x + rmsnorm(f, g_post_ffn[l])
    return x


def setup_inputs(seed=0):
    out = dict(first_inputs(seed))
    for name, value in second_inputs(seed + 1).items():
        if name != "x":
            out[name + "_2"] = value
    return out


def reference(
    x, c, positions, w_ada, b_ada, g_pre_mix, g_post_mix, g_pre_ffn, g_post_ffn, w_in, w_pool,
    b_pool, pool_scale, w_out, w_up, conv_w, conv_b, w_down, mem_2, rel_bias_2, g_pre_mix_2,
    g_post_mix_2, g_pre_ffn_2, g_post_ffn_2, g_mem_2, w_in_2, b_gate_2, conv_mix_w_2,
    w_conv_out_2, w_attn_out_2, w_mem_kv_2, w_mem_out_2, w_out_2, w_up_2, ffn_conv_w_2,
    ffn_conv_b_2, w_down_2,
):
    x = first_block(
        x, c, positions, w_ada, b_ada, g_pre_mix, g_post_mix, g_pre_ffn, g_post_ffn, w_in,
        w_pool, b_pool, pool_scale, w_out, w_up, conv_w, conv_b, w_down,
    )
    return second_block(
        x, mem_2, rel_bias_2, g_pre_mix_2, g_post_mix_2, g_pre_ffn_2, g_post_ffn_2, g_mem_2,
        w_in_2, b_gate_2, conv_mix_w_2, w_conv_out_2, w_attn_out_2, w_mem_kv_2, w_mem_out_2,
        w_out_2, w_up_2, ffn_conv_w_2, ffn_conv_b_2, w_down_2,
    )


_drawn_inputs = setup_inputs


def setup_inputs(seed=0):
    import zlib

    import numpy as np

    out = dict(_drawn_inputs(seed))
    spreads = {}
    factors = {'b_pool': 3.358,
     'conv_b': 5.073,
     'g_mem_2': 8.0,
     'b_gate_2': 8.0,
     'ffn_conv_b_2': 7.692,
     'rel_bias_2': 8.0}
    for name, (base, spread) in spreads.items():
        noise = np.random.default_rng([zlib.crc32(name.encode()), seed]).standard_normal(out[name].shape)
        drawn = base * np.exp(spread * noise) if base else spread * noise
        out[name] = __import__('jax').numpy.asarray(drawn.astype(out[name].dtype))
    for name, factor in factors.items():
        out[name] = (out[name] * factor).astype(out[name].dtype)
    return out
```

```python
from contextlib import ExitStack

import concourse.bass as bass
from concourse import mybir

F32 = mybir.dt.float32
F32R = mybir.dt.float32r
I32 = mybir.dt.int32
ACT = mybir.ActivationFunctionType
ALU = mybir.AluOpType
X = mybir.AxisListType.X

P = 128
D = 1024
S = 512
KD = D // P
TT = S // P
UC = 256
D_FF = 2816
KF = D_FF // P
FF_PAIRS = D_FF // UC
EPS = 1e-6
NEG = -1e30
DH = 64
GROUPS = 3
GH = 4
POOL_PAD = 16
WINDOWS = (2, 4, 8, 16)
HEADS2 = 8
MEM = 256
MEM_HEADS = 4
TWO_PI = 6.283185307179586
MAGIC = 12582912.0
BUCKETS = 32
REL = S + P

C_ID, C_PREV, C_CAUSAL, C_BLOCK = 0, 128, 256, 384
C_FREQ, C_SEL, C_RC, C_RW, C_END = 512, 520, 776, 808, 810

VEC = {
    "c": (0, 0, 8), "b_ada": (0, 8, 48), "g_pre_mix": (0, 56, 8), "g_post_mix": (0, 64, 8),
    "g_pre_ffn": (0, 72, 8), "g_post_ffn": (0, 80, 8), "b_pool": (0, 88, 2), "pool_scale": (0, 90, 2),
    "b_gate_2": (0, 92, 24),
    "conv_w": (1, 0, 66), "conv_b": (1, 66, 22), "g_pre_mix_2": (1, 88, 8), "g_post_mix_2": (1, 96, 8),
    "g_pre_ffn_2": (1, 104, 8), "g_post_ffn_2": (1, 112, 8), "g_mem_2": (1, 120, 8),
    "ffn_conv_w_2": (2, 0, 88), "conv_mix_w_2": (2, 88, 12),
    "ffn_conv_w_2b": (3, 0, 44), "ffn_conv_b_2": (3, 44, 44),
}
TABLE_ROWS = (116, 128, 100, 88)

D_IN, D_OUT, D_UP1, D_DOWN1 = 0, 10, 14, 36
D_IN2, D_BR0, D_BR1, D_KV, D_BR2 = 52, 64, 72, 80, 86
D_OUT2, D_UP2, D_DOWN2, D_END = 94, 98, 120, 136
ADA_FIRST, ADA_REST = 8, 16
DOWN_K = (6, 6, 5, 5)
DOWN_K0 = (0, 6, 12, 17)


def raw_index(d):
    return d + ADA_FIRST + (ADA_REST if d >= D_OUT else 0)


def bank_use(d):
    if d <= D_UP1:
        return d // 2
    if d < D_IN2:
        return D_UP1 // 2 + (d - D_DOWN1) // 8
    if d <= D_UP2:
        return D_UP1 // 2 + 2 + (d - D_IN2) // 2
    return D_UP1 // 2 + 2 + (D_UP2 - D_IN2) // 2 + (d - D_DOWN2) // 8


def pair_of(d):
    if D_DOWN1 <= d < D_IN2:
        return (d - D_DOWN1) // 4 % 2
    if d >= D_DOWN2:
        return (d - D_DOWN2) // 4 % 2
    return d % 2


TILES1 = [(g, b, 2 if g == 0 and b > 0 else 1) for g in range(GROUPS) for b in range(TT)]
TILES2 = [("self", i, h, i + 1) for i in range(TT) for h in range(HEADS2)]
TILES3 = [("mem", i, h, MEM // P) for i in range(TT) for h in range(MEM_HEADS)]
TILES23 = TILES2 + TILES3

(N_PRE1, N_POST1, N_PREF1, N_POSTF1, N_PRE2, N_MEM, N_POST2, N_PREF2, N_POSTF2) = range(9)
SPLITS = {N_PRE1: 0, N_PREF1: 1, N_PRE2: 2, N_MEM: 3, N_PREF2: 4}
RESID = {N_POST1: 0, N_POSTF1: 1, N_POST2: 2, N_POSTF2: 3}


def build(nc, a, out):
    ctx = ExitStack()
    with ctx:
        def sb(name, shape, dt=F32):
            return ctx.enter_context(nc.sbuf_tensor(name, shape, dt))

        def sem(name):
            return ctx.enter_context(nc.semaphore(name))

        K = sb("K", [P, C_END])
        ones = sb("ones", [P, P])
        vec = sb("vec", [P, 4, P])
        mod = sb("mod", [P, 48])
        colA = sb("colA", [P, 4, KD])
        small = sb("small", [P, 64])
        xT = sb("xT", [P, KD, S])
        hH = sb("hH", [P, KD, S], F32R)
        hL = sb("hL", [P, KD, S], F32R)
        raw = sb("raw", [P, 2, KD, UC])
        WH = sb("WH", [P, 2, KD, UC], F32R)
        WL = sb("WL", [P, 2, KD, UC], F32R)
        base = (nc.sbuf_base + 31) // 32 * 32
        room = nc.sbuf_usable_end - base
        ctx.enter_context(nc.sbuf_tensor("arena", [P, (room - 64) // 4], F32))

        def at(name, shape, kib, dt=F32):
            free = 4
            for n in shape[1:]:
                free *= n
            assert kib * 1024 + free <= room - 64, (name, kib * 1024 + free, room)
            return nc.alloc_sbuf_tensor_at(name, shape, dt, offset=base + int(kib * 1024))

        sq = at("sq", [P, 2, S], 0)
        nt = at("nt", [P, 2, S], 4)
        vrow = at("vrow", [P, 4, P], 8)
        xtok = at("xtok", [P, TT, D], 12)
        posi = at("posi", [P, GROUPS * TT], 30, I32)
        posf = at("posf", [P, GROUPS * TT], 30.5)
        trig = at("trig", [P, 5, GROUPS * TT, 8], 31)
        u = at("u", [P, 2, POOL_PAD + S], 8)
        win = at("win", [P, 2, POOL_PAD + S], 12.5)
        qtok = at("qtok", [P, 2, TT, UC], 17)
        rope = at("rope", [P, 4, TT, GH, 8], 25)
        wpool = at("wpool", [P, 2, DH], 28)
        md = at("md", [P, len(TILES1), 2, GH], 28.5)
        qT = at("qT", [P, 6, S], 33)
        kT = at("kT", [P, 6, S], 45)
        V1 = at("V1", [P, TT, GROUPS, UC], 57)
        S1 = at("S1", [P, 2, 2, 2, 2 * P], 69)
        PT1 = at("PT1", [P, 2, 2, GH * P], 77)
        oT = at("oT", [P, 6, S], 85)
        stats = at("stats", [GH, 2, GROUPS, S], 0)
        cosT = at("cosT", [P, GROUPS, TT, 8], 98)
        sinT = at("sinT", [P, GROUPS, TT, 8], 98.5)
        negm = at("negm", [P, len(TILES1), GH], 99)
        alpha = at("alpha", [GH, GROUPS, S], 17)
        amax = at("amax", [GH, 2, S], 23)
        comb = at("comb", [P, 3, S], 69)
        y1 = at("y1", [P, KD, S], 33)
        hidH = at("hidH", [P, KF, S], 0, F32R)
        hidL = at("hidL", [P, KF, S], 44, F32R)
        act = at("act", [P, 4, S], 88)
        yff = at("yff", [P, KD, S], 88)
        hot = at("hot", [BUCKETS, 2 * REL], 8)
        rel = at("rel", [BUCKETS, HEADS2], 13.25)
        rrow = at("rrow", [HEADS2, REL], 13.5)
        cc = at("cc", [P, 4, S + 2], 8)
        md2 = at("md2", [P, 3, len(TILES23)], 17)
        bufAH = at("bufAH", [P, 4, S], 20, F32R)
        bufAL = at("bufAL", [P, 4, S], 28, F32R)
        bufBH = at("bufBH", [P, 4, S], 36, F32R)
        bufBL = at("bufBL", [P, 4, S], 44, F32R)
        merged = at("merged", [P, KD, S], 52)
        sg = at("sg", [P, 2, S], 68)
        q2 = at("q2", [P, 4, S], 72)
        k2 = at("k2", [P, 4, S], 80)
        V2 = at("V2", [P, TT, HEADS2 * DH], 88)
        W0 = at("W0", [P, 4, S], 8)
        W1 = at("W1", [P, 4, S], 96)
        S2 = at("S2", [P, 2, S], 0)
        PT2 = at("PT2", [P, 2, S], 4)
        memtok = at("memtok", [P, MEM // P, D], 72)
        memT = at("memT", [P, KD, MEM], 80)
        mk = at("mk", [P, MEM_HEADS, MEM], 88)
        mv = at("mv", [P, MEM // P, MEM_HEADS * P], 92)
        qm = at("qm", [P, 4, S], 8)
        y2 = at("y2", [P, KD, S], 72)
        otok = at("otok", [P, TT, D], 8)
        memH = bufAH[:].rearrange("p c (e m) -> p (c e) m", e=2)
        memL = bufAL[:].rearrange("p c (e m) -> p (c e) m", e=2)

        ps = ctx.enter_context(nc.psum_tensor("ps", [P, 8, 512], F32))
        scratch = nc.dram_tensor("bias_rows", (HEADS2, P, REL), F32, kind="Internal")

        ident = K[:, C_ID:C_ID + P]

        def v(name, n=0, count=1):
            t, r, _ = VEC[name]
            if isinstance(n, int):
                return vec[:, t, r + n:r + n + count]
            return vec[:, t, bass.ds(n + r, count)]

        k_loaded = sem("k_loaded")
        vec_loaded = sem("vec_loaded")
        x_loaded = sem("x_loaded")
        pos_loaded = sem("pos_loaded")
        wpool_loaded = sem("wpool_loaded")
        raw_loaded = [sem("raw_loaded0"), sem("raw_loaded1")]
        ada_used = sem("ada_used")
        hi_done = sem("hi_done")
        lo_done = sem("lo_done")
        pe_seg = sem("pe_seg")
        banks_read = [sem("banks_read0"), sem("banks_read1")]
        ones_ready = sem("ones_ready")
        vec_turned = sem("vec_turned")
        vec_ready = sem("vec_ready")
        x_turned = sem("x_turned")
        x_ready = sem("x_ready")
        silu_exp = sem("silu_exp")
        cact_ready = sem("cact_ready")
        angle_ready = sem("angle_ready")
        trig_ready = sem("trig_ready")
        mod_ready = sem("mod_ready")
        sq_ready = sem("sq_ready")
        ss_added = sem("ss_added")
        var_ready = sem("var_ready")
        std_ready = sem("std_ready")
        rstd_ready = sem("rstd_ready")
        scaled = sem("scaled")
        h_hi = sem("h_hi")
        h_lo = sem("h_lo")
        delta_ready = sem("delta_ready")
        x_added = sem("x_added")
        rope_done = sem("rope_done")
        turned = sem("turned")
        turn_read = sem("turn_read")
        s_done = sem("s_done")
        s_read = sem("s_read")
        negm_ready = sem("negm_ready")
        exp_done = sem("exp_done")
        pt_done = sem("pt_done")
        pt_read = sem("pt_read")
        pv_done = sem("pv_done")
        pv_read = sem("pv_read")
        pool_mixed = sem("pool_mixed")
        pool_done = sem("pool_done")
        pool_val = sem("pool_val")
        cat_hi = sem("cat_hi")
        cat_lo = sem("cat_lo")
        gap_ready = sem("gap_ready")
        gap_exp = sem("gap_exp")
        alpha_ready = sem("alpha_ready")
        alpha_spread = sem("alpha_spread")
        attn_ready = sem("attn_ready")
        seeded = sem("seeded")
        gate_conv = sem("gate_conv")
        val_conv = sem("val_conv")
        gelu_done = sem("gelu_done")
        hid_ready = sem("hid_ready")
        hid_hi = sem("hid_hi")
        hid_lo = sem("hid_lo")
        hot_loaded = sem("hot_loaded")
        rel_done = sem("rel_done")
        rrow_ready = sem("rrow_ready")
        rrow_stored = sem("rrow_stored")
        bias_loaded = sem("bias_loaded")
        pads_zero = sem("pads_zero")
        conv_y = sem("conv_y")
        conv_hi = sem("conv_hi")
        conv_lo = sem("conv_lo")
        s2_done = sem("s2_done")
        s2_read = sem("s2_read")
        negm2_ready = sem("negm2_ready")
        exp2_done = sem("exp2_done")
        p2_scaled = sem("p2_scaled")
        pt2_done = sem("pt2_done")
        pt2_read = sem("pt2_read")
        pv2_done = sem("pv2_done")
        o2_hi = sem("o2_hi")
        o2_lo = sem("o2_lo")
        sig_done = sem("sig_done")
        merged_ready = sem("merged_ready")
        m_hi = sem("m_hi")
        m_lo = sem("m_lo")
        mem_loaded = sem("mem_loaded")
        mem_turned = sem("mem_turned")
        mem_ready = sem("mem_ready")
        out_turned = sem("out_turned")
        out_copied = sem("out_copied")
        out_stored = sem("out_stored")
        act_own = sem("act_own")
        dve_own = sem("dve_own")

        def rows(w, k0, nk, c0):
            return w.rearrange("(k p) n -> p k n", p=P)[:, k0:k0 + nk, c0:c0 + UC]

        def unit_source(d):
            if d < D_OUT:
                if d == 0:
                    return rows(a["w_in"], 0, KD, 0), KD
                g, part = (d - 1) // 3, (d - 1) % 3
                return rows(a["w_in"], 0, KD, UC + part * 768 + g * UC), KD
            if d < D_UP1:
                return rows(a["w_out"], 0, 4, (d - D_OUT) * UC), 4
            if D_DOWN1 <= d < D_IN2 or d >= D_DOWN2:
                w, r = (a["w_down"], d - D_DOWN1) if d < D_IN2 else (a["w_down_2"], d - D_DOWN2)
                g, q = r // 4, r % 4
                return rows(w, DOWN_K0[q], DOWN_K[q], g * UC), DOWN_K[q]
            if D_UP1 <= d < D_DOWN1 or D_UP2 <= d < D_DOWN2:
                w, r = (a["w_up"], d - D_UP1) if d < D_IN2 else (a["w_up_2"], d - D_UP2)
                return rows(w, 0, KD, r % 2 * D_FF + r // 2 * UC), KD
            if d < D_BR0:
                r = d - D_IN2
                col = (512, 1024, 0, 1536, 2048, 2560)[r // 2] + r % 2 * UC
                return rows(a["w_in_2"], 0, KD, col), KD
            if D_KV <= d < D_KV + 4:
                return rows(a["w_mem_kv_2"], 0, KD, (d - D_KV) * UC), KD
            if D_KV + 4 <= d < D_BR2:
                return rows(a["w_in_2"], 0, KD, 3072 + (d - D_KV - 4) * UC), KD
            if d < D_OUT2:
                br, d0, w = next((i, x, y) for i, x, y in (
                    (2, D_BR2, a["w_mem_out_2"]), (1, D_BR1, a["w_attn_out_2"]), (0, D_BR0, a["w_conv_out_2"])) if d >= x)
                j, r = (d - d0) // 2, (d - d0) % 2
                if r == 0:
                    return rows(a["w_in_2"], 0, KD, 3584 + br * D + j * UC), KD
                return rows(w, 0, 4, j * UC), 4
            return rows(a["w_out_2"], 0, KD, (d - D_OUT2) * UC), KD

        def split_chunks(d):
            if D_UP1 <= d < D_DOWN1 + 2 or D_UP2 <= d < D_DOWN2 + 2:
                return KD
            return unit_source(d)[1]

        def tokens(t, k, g, b):
            if g == 0:
                return t[:, k, b * P:(b + 1) * P]
            return t[:, k, :].rearrange("p (i r) -> p r i", r=TT)[:, b, :]

        def key_blocks(n):
            return sum(t[2] for t in TILES1[:n])

        def pairs_before(n):
            return sum(1 for t in TILES23[:n] if t[0] == "mem" or t[2] % 2 == 1)

        steps = [("start",), ("ada", 0), ("split", 0), ("split", 1), ("norm", N_PRE1), ("apply", N_PRE1)]
        e = 0
        for d in range(D_IN, D_OUT):
            steps += [("seg", d, 0), ("seg", d, 1)]
            if d + 2 < D_OUT:
                steps += [("split", d + 2)]
            steps += [("evac_in", d)]
            if d >= 2 and (d - 1) % 3 in (1, 2):
                steps += [("turn", e)]
                e += 1
        steps += [("ada", 1), ("split", D_OUT), ("split", D_OUT + 1), ("pool",)]
        steps += [("front", 0)]
        for n in range(len(TILES1)):
            if n + 1 < len(TILES1):
                steps += [("front", n + 1)]
            steps += [("mid", n), ("back", n)]
        steps += [("combine",)]
        for d in range(D_OUT, D_UP1):
            steps += [("seg", d, 0), ("seg", d, 1), ("split", d + 2), ("evac_y", d)]
        steps += [("norm", N_POST1), ("resid", N_POST1), ("norm", N_PREF1), ("apply", N_PREF1), ("up", 0)]
        for d in range(D_DOWN1, D_IN2):
            steps += [("seg", d, 0), ("seg", d, 1), ("split", d + 2)]
            if (d - D_DOWN1) % 4 == 3:
                steps += [("evac_y", d)]
        steps += [("norm", N_POSTF1), ("resid", N_POSTF1), ("bias_rows",), ("norm", N_PRE2), ("apply", N_PRE2)]
        for d in range(D_IN2, D_BR0):
            steps += [("seg", d, 0), ("seg", d, 1), ("split", d + 2), ("evac_in2", d)]
        steps += [("bias_load",)]

        def branch(d0):
            out = []
            for d in range(d0, d0 + 8):
                out += [("seg", d, 0), ("seg", d, 1), ("split", d + 2), ("evac_br", d)]
            return out

        def attend(first, last):
            out = [("front2", first)]
            for n in range(first, last):
                if n + 1 < last:
                    out += [("front2", n + 1)]
                out += [("mid2", n), ("back2", n)]
            return out

        steps += branch(D_BR0)
        steps += attend(0, len(TILES2))
        steps += [("mem_load",)]
        steps += branch(D_BR1)
        steps += [("mem_turn",), ("norm", N_MEM), ("apply", N_MEM)]
        for d in range(D_KV, D_BR2):
            steps += [("seg", d, 0), ("seg", d, 1), ("split", d + 2), ("evac_kv", d)]
        steps += attend(len(TILES2), len(TILES23))
        steps += branch(D_BR2)
        steps += [("merge",)]
        for d in range(D_OUT2, D_UP2):
            steps += [("seg", d, 0), ("seg", d, 1), ("split", d + 2), ("evac_y", d)]
        steps += [("norm", N_POST2), ("resid", N_POST2), ("norm", N_PREF2), ("apply", N_PREF2), ("up", 1)]
        for d in range(D_DOWN2, D_END):
            steps += [("seg", d, 0), ("seg", d, 1)]
            if d + 2 < D_END:
                steps += [("split", d + 2)]
            if (d - D_DOWN2) % 4 == 3:
                steps += [("evac_y", d)]
        steps += [("norm", N_POSTF2), ("resid", N_POSTF2), ("finish",)]

        def walk(handlers):
            for step in steps:
                f = handlers.get(step[0])
                if f is not None:
                    f(*step[1:])

        def y_of(d):
            if d < D_UP1:
                return y1, 2 * (d - D_OUT)
            if d < D_IN2:
                return yff, 2 * ((d - D_DOWN1) // 4)
            if d < D_UP2:
                return y2, 2 * (d - D_OUT2)
            return yff, 2 * ((d - D_DOWN2) // 4)

        def banks(d):
            p = pair_of(d)
            return ps[:, 2 * p:2 * p + 2, :]

        norm_source = {
            N_PRE1: (xT, S), N_POST1: (y1, S), N_PREF1: (xT, S), N_POSTF1: (yff, S), N_PRE2: (xT, S),
            N_MEM: (memT, MEM), N_POST2: (y2, S), N_PREF2: (xT, S), N_POSTF2: (yff, S)}
        gains = {
            N_PRE1: colA[:, 0, :], N_POST1: colA[:, 1, :], N_PREF1: colA[:, 2, :], N_POSTF1: colA[:, 3, :],
            N_PRE2: v("g_pre_mix_2", 0, 8), N_MEM: v("g_mem_2", 0, 8), N_POST2: v("g_post_mix_2", 0, 8),
            N_PREF2: v("g_pre_ffn_2", 0, 8), N_POSTF2: v("g_post_ffn_2", 0, 8)}
        shifts = {N_PRE1: mod[:, 0:8], N_PREF1: mod[:, 24:32]}
        y_units = {N_POST1: D_OUT, N_POST2: D_OUT2, N_POSTF1: D_DOWN1, N_POSTF2: D_DOWN2}

        def tile2(n):
            kind, i, h, nb = TILES23[n]
            return (kind, i, h, nb, h // 2, DH * (h % 2)) if kind == "self" else (kind, i, h, nb, h, 0)

        block = ctx.enter_context(nc.Block())

        @block.sync
        def _(sp):
            def slot_free(r):
                o = r - 2
                if o < 0:
                    return
                if o < ADA_FIRST:
                    sp.wait_ge(ada_used, o + 1)
                elif o < raw_index(D_OUT - 1) + 1:
                    sp.wait_ge(lo_done, o - ADA_FIRST + 1)
                elif o < raw_index(D_OUT):
                    sp.wait_ge(ada_used, o - D_OUT + 1)
                else:
                    sp.wait_ge(lo_done, o - ADA_FIRST - ADA_REST + 1)

            def load(r, src, nk):
                slot_free(r)
                sp.dma_start(raw[:, r % 2, 0:nk, :], src).then_inc(raw_loaded[r % 2], 16)

            def ada(first, count, r0):
                for i in range(count):
                    load(r0 + i, rows(a["w_ada"], 0, KD, (first + i) * UC), KD)

            def up(w, d0):
                cols = w.rearrange("(k p) n -> p k n", p=P)
                with sp.Fori(0, FF_PAIRS) as j:
                    for half in range(2):
                        sp.wait_ge(lo_done, j * 2 + (d0 + half - 1))
                        sp.dma_start(raw[:, half, :, :], cols[:, :, bass.ds(j * UC + half * D_FF, UC)]
                                     ).then_inc(raw_loaded[half], 16)

            def dense(d0, d1):
                for d in range(d0, d1):
                    src, nk = unit_source(d)
                    load(raw_index(d), src, nk)

            ada(0, ADA_FIRST, 0)
            dense(D_IN, D_OUT)
            ada(ADA_FIRST, ADA_REST, raw_index(D_OUT - 1) + 1)
            dense(D_OUT, D_UP1)
            up(a["w_up"], D_UP1)
            dense(D_DOWN1, D_UP2)
            up(a["w_up_2"], D_UP2)
            dense(D_DOWN2, D_END)
            for t in range(TT):
                sp.wait_ge(out_copied, t + 1)
                sp.dma_start(out[t * P:(t + 1) * P, :], otok[:, t, :]).then_inc(out_stored, 16)
            sp.wait_ge(out_stored, 16 * TT)

        @block.gpsimd
        def _(pool):
            def cut(d):
                nk = split_chunks(d)
                pool.wait_ge(hi_done, d + 1)
                pool.tensor_tensor(WL[:, d % 2, 0:nk, :], raw[:, d % 2, 0:nk, :],
                                   WH[:, d % 2, 0:nk, :].bitcast(F32), ALU.subtract).then_inc(lo_done, 1)

            def resid(n):
                for k in range(KD):
                    m = KD * RESID[n] + k
                    pool.wait_ge(delta_ready, m + 1)
                    pool.tensor_tensor(xT[:, k, :], xT[:, k, :], nt[:, k % 2, :], ALU.add).then_inc(x_added, 1)

            def up(f):
                d0 = (D_UP1, D_UP2)[f]
                with pool.Fori(0, FF_PAIRS) as j:
                    for half in range(2):
                        pool.wait_ge(hi_done, j * 2 + (d0 + 2 + half + 1))
                        pool.tensor_tensor(WL[:, half, :, :], raw[:, half, :, :],
                                           WH[:, half, :, :].bitcast(F32), ALU.subtract).then_inc(lo_done, 1)

            walk({"split": cut, "resid": resid, "up": up})

        @block.scalar
        def _(sc):
            own = [0]

            def link(ins):
                own[0] += 1
                ins.then_inc(act_own, 1)
                sc.wait_ge(act_own, own[0])

            def start():
                sc.dma_start(K[:], a["table"]).then_inc(k_loaded, 16)
                for name, (t, r, n) in VEC.items():
                    src = {"ffn_conv_w_2b": "ffn_conv_w_2"}.get(name, name)
                    flat = a[src]
                    off = 88 if name == "ffn_conv_w_2b" else 0
                    sc.dma_start(vrow[r:r + n, t, :], flat[off:off + n, :]).then_inc(vec_loaded, 16)
                for t in range(TT):
                    sc.dma_start(xtok[:, t, :], a["x"][t * P:(t + 1) * P, :]).then_inc(x_loaded, 16)
                sc.dma_start(posi[:], a["positions"]).then_inc(pos_loaded, 16)
                sc.dma_start(wpool[:], a["w_pool"].rearrange("(m g) c d -> (g c) m d", g=2)).then_inc(wpool_loaded, 16)
                sc.wait_ge(vec_ready, 4)
                sc.activation(small[:, 0:8], v("c", 0, 8), ACT.Exp, scale=-1.0).then_inc(silu_exp, 1)
                sc.wait_ge(angle_ready, 2)
                sc.activation(sinT[:].rearrange("p g t f -> p (g t) f"), trig[:, 2, :, :], ACT.Sin).then_inc(trig_ready, 1)
                sc.activation(cosT[:].rearrange("p g t f -> p (g t) f"), trig[:, 3, :, :], ACT.Sin).then_inc(trig_ready, 1)

            def split(d):
                r = raw_index(d)
                nk = split_chunks(d)
                sc.wait_ge(raw_loaded[r % 2], 16 * (r // 2 + 1))
                if d >= 2:
                    sc.wait_ge(pe_seg, 2 * (d - 2) + 2)
                sc.activation(WH[:, d % 2, 0:nk, :], raw[:, d % 2, 0:nk, :], ACT.Copy).then_inc(hi_done, 1)

            def norm(n):
                src, w = norm_source[n]
                for k in range(KD):
                    m = KD * n + k
                    if n == N_PRE1:
                        sc.wait_ge(x_ready, k + 1)
                    elif n == N_MEM:
                        sc.wait_ge(mem_ready, k + 1)
                    elif n in y_units:
                        d = y_units[n] + (k // 2 if n in (N_POST1, N_POST2) else 4 * (k // 2))
                        sc.wait_ge(banks_read[pair_of(d)], bank_use(d) + 1)
                    else:
                        sc.wait_ge(x_added, KD * RESID[n - 1] + k + 1)
                    if m >= 2:
                        sc.wait_ge(ss_added, m - 1)
                    sc.activation(sq[:, k % 2, 0:w], src[:, k, :], ACT.Square).then_inc(sq_ready, 1)
                sc.wait_ge(var_ready, n + 1)
                sc.activation(nt[:, 1, 0:w], nt[:, 0, 0:w], ACT.Sqrt).then_inc(std_ready, 1)

            def apply(n):
                w = norm_source[n][1]
                dst = memH if n == N_MEM else hH
                for k in range(KD):
                    sc.wait_ge(scaled, KD * SPLITS[n] + k + 1)
                    if n in shifts:
                        ins = sc.activation(dst[:, k, :], nt[:, k % 2, 0:w], ACT.Identity, bias=shifts[n][:, k:k + 1])
                    else:
                        ins = sc.activation(dst[:, k, :], nt[:, k % 2, 0:w], ACT.Copy)
                    ins.then_inc(h_hi, 1)

            def evac_in(d):
                sc.wait_ge(pe_seg, 2 * d + 2)
                if d == 0:
                    sc.wait_ge(pads_zero, 1)
                    ins = sc.activation(u[:, :, POOL_PAD:], banks(d), ACT.Copy)
                else:
                    g, part = (d - 1) // 3, (d - 1) % 3
                    src = banks(d).rearrange("p b (t n) -> p (b t) n", t=2)
                    if part == 2:
                        ins = sc.activation(V1[:, :, g, :], src, ACT.Copy)
                    else:
                        e = 2 * g + part
                        if e >= 2:
                            sc.wait_ge(turned, 2 * (e - 1))
                        ins = sc.activation(qtok[:, e % 2, :, :], src, ACT.Copy)
                ins.then_inc(banks_read[pair_of(d)], 1)

            def turn(e):
                dst = qT if e % 2 == 0 else kT
                for hp in range(2):
                    sc.wait_ge(turned, 2 * e + hp + 1)
                    sc.activation(dst[:, 2 * (e // 2) + hp, :], ps[:, 6 + hp, :], ACT.Copy).then_inc(turn_read, 1)

            def pool_step():
                for m in range(2):
                    sc.wait_ge(pool_done, m + 1)
                    for half in range(2):
                        r = slice(64 * half, 64 * half + 64)
                        ins = sc.activation(win[r, m, 0:S], ps[r, 2 * m + half, :], ACT.Identity,
                                            bias=small[r, 16 + m:17 + m], scale=v("pool_scale", m)[r, :])
                        ins.then_inc(pool_val, 1)
                    sc.wait_ge(pool_val, 2 * m + 2)
                    sc.activation(hH[:, m, :], win[:, m, 0:S], ACT.Copy).then_inc(cat_hi, 1)

            def front(n):
                sc.wait_ge(negm_ready, n + 1)
                w = P * TILES1[n][2]
                for x in range(GH):
                    t = S1[:, n % 2, x // 2, x % 2, 0:w]
                    sc.activation(t, t, ACT.Exp, bias=negm[:, n, x:x + 1], scale=DH ** -0.5,
                                  accum_out=md[:, n, 1, x:x + 1]).then_inc(exp_done, 1)

            def mid(n):
                if n >= 2:
                    sc.wait_ge(pv_done, n - 1)
                for kb in range(TILES1[n][2]):
                    sc.wait_ge(pt_done, key_blocks(n) + kb + 1)
                    sc.activation(PT1[:, n % 2, kb, :], ps[:, 6, :], ACT.Copy).then_inc(pt_read, 1)

            def combine():
                sc.wait_ge(gap_ready, 1)
                sc.activation(alpha[:], alpha[:], ACT.Exp, scale=DH ** -0.5).then_inc(gap_exp, 1)
                for hp in range(2):
                    sc.wait_ge(attn_ready, hp + 1)
                    sc.activation(hH[:, 2 + hp, :], comb[:, 0, :], ACT.Copy).then_inc(cat_hi, 1)

            def evac_y(d):
                sc.wait_ge(pe_seg, 2 * d + 2)
                y, c = y_of(d)
                sc.activation(y[:, c:c + 2, :], banks(d), ACT.Copy).then_inc(banks_read[pair_of(d)], 1)

            def up(f):
                d0 = (D_UP1, D_UP2)[f]
                t0 = 4 * FF_PAIRS if f else 0
                with sc.Fori(0, FF_PAIRS) as j:
                    def cut(half):
                        d = d0 + 2 + half
                        sc.wait_ge(raw_loaded[half], j * 16 + 16 * (raw_index(d) // 2 + 1))
                        sc.wait_ge(pe_seg, j * 4 + 2 * (d - 2) + 2)
                        sc.activation(WH[:, half, :, :], raw[:, half, :, :], ACT.Copy).then_inc(hi_done, 1)

                    def seed(m, half):
                        if f == 0:
                            w2, b = v("conv_w", j * 2 + (44 + m)), v("conv_b", j * 2 + m)
                        else:
                            c = j * 2 + (22 * half + m)
                            w2, b = v("ffn_conv_w_2b", c), v("ffn_conv_b_2", c)
                        sc.activation(act[:, 2 * half + m, :], ps[:, 2 * half + m, :], ACT.Identity,
                                      bias=b, scale=w2).then_inc(seeded, 1)

                    sc.wait_ge(hid_lo, j * 2 + (2 + 2 * FF_PAIRS * f))
                    sc.wait_ge(pe_seg, j * 4 + 2 * d0 + 1)
                    seed(0, 0)
                    sc.wait_ge(pe_seg, j * 4 + 2 * d0 + 2)
                    seed(1, 0)
                    cut(0)
                    for m in range(2):
                        sc.wait_ge(gate_conv, j * 2 + (m + 3 + 2 * FF_PAIRS * f))
                        sc.activation(act[:, m, :], act[:, m, :], ACT.Gelu_apprx_tanh).then_inc(gelu_done, 1)
                    if f == 1:
                        for m in range(2):
                            sc.wait_ge(pe_seg, j * 4 + 2 * d0 + 3 + m)
                            seed(m, 1)
                    cut(1)
                    for m in range(2):
                        sc.wait_ge(hid_ready, j * 2 + (m + 3 + 2 * FF_PAIRS * f))
                        sc.activation(hidH[:, bass.ds(j * 2 + m, 1), :], act[:, m:m + 1, :], ACT.Copy).then_inc(hid_hi, 1)

            def bias_rows():
                sc.wait_ge(x_added, KD * RESID[N_POSTF1] + KD)
                sc.dma_start(hot[:], a["hot"]).then_inc(hot_loaded, 16)
                sc.dma_start(rel[:], a["rel_bias_2"]).then_inc(hot_loaded, 16)
                sc.wait_ge(rrow_ready, 2)
                sc.dma_start(scratch.ap(), rrow[:].unsqueeze(1).broadcast_to([HEADS2, P, REL])).then_inc(rrow_stored, 16)

            def evac_in2(d):
                r = d - D_IN2
                kind, j = r // 2, r % 2
                if kind == 0:
                    sc.wait_ge(pe_seg, 2 * d + 2)
                    sc.wait_ge(rrow_stored, 16)
                    sc.activation(cc[:, 2 * j:2 * j + 2, 2:], banks(d), ACT.Copy).then_inc(banks_read[d % 2], 1)
                elif kind == 2:
                    for m in range(2):
                        c = 2 * j + m
                        sc.wait_ge(*((banks_read[j], bank_use(d) + 1) if m else (conv_y, j + 1)))
                        sc.activation(bufAH[:, c, :], sq[:, m, :], ACT.Copy).then_inc(conv_hi, 1)
                elif kind >= 3:
                    sc.wait_ge(pe_seg, 2 * d + 2)
                    if kind == 5:
                        ins = sc.activation(V2[:, :, UC * j:UC * j + UC],
                                            banks(d).rearrange("p b (t n) -> p (b t) n", t=2), ACT.Copy)
                    else:
                        ins = sc.activation((q2, k2)[kind - 3][:, 2 * j:2 * j + 2, :], banks(d), ACT.Copy)
                    ins.then_inc(banks_read[d % 2], 1)

            def bias_load():
                sc.wait_ge(conv_lo, 4)
                for i, w in enumerate((W0, W1)):
                    src = bass.AP(tensor=scratch, offset=4 * i * P * REL + P - 1, ap=[[REL - 1, P], [P * REL, 4], [1, S]])
                    sc.dma_start(w[:], src).then_inc(bias_loaded, 16)

            def evac_br(d):
                br = next(i for i, d0 in ((2, D_BR2), (1, D_BR1), (0, D_BR0)) if d >= d0)
                j, r = (d - (D_BR0, D_BR1, D_BR2)[br]) // 2, (d - D_BR0) % 2
                if r:
                    return
                for m in range(2):
                    c = 2 * j + m
                    sc.wait_ge(pe_seg, 2 * d + 1 + m)
                    n = 8 * br + c
                    if n >= 2:
                        sc.wait_ge(merged_ready, n - 1)
                    ins = sc.activation(sg[:, m, :], ps[:, 2 * pair_of(d) + m, :], ACT.Sigmoid,
                                        bias=v("b_gate_2", 8 * br + c))
                    if m == 0:
                        link(ins)
                ins.then_inc(banks_read[pair_of(d)], 1)

            def front2(n):
                kind, i, h, nb, _, _ = tile2(n)
                sc.wait_ge(negm2_ready, n + 1)
                if kind == "self":
                    t, scale = S2[:, n % 2, 0:P * nb], 1.0
                    src = t
                else:
                    t, scale = S2[:, n % 2, 0:P * nb], P ** -0.5
                    src = ps[:, 4 + n % 2, 0:P * nb]
                sc.activation(t, src, ACT.Exp, bias=md2[:, 0, n:n + 1], scale=scale,
                              accum_out=md2[:, 1, n:n + 1]).then_inc(exp2_done, 1)

            def mid2(n):
                nb = tile2(n)[3]
                sc.wait_ge(pt2_done, n + 1)
                if n >= 2:
                    sc.wait_ge(pv2_done, n - 1)
                sc.activation(PT2[:, n % 2, 0:P * nb], ps[:, 6, 0:P * nb], ACT.Copy).then_inc(pt2_read, 1)

            def back2(n):
                kind, i, h, _, c, row = tile2(n)
                if kind == "self" and row == 0:
                    return
                sc.wait_ge(pv2_done, n + 1)
                dst = bufBH if kind == "self" else bufAH
                sc.activation(dst[:, c, i * P:(i + 1) * P], ps[:, 7, 0:P], ACT.Copy).then_inc(o2_hi, 1)

            def mem_load():
                sc.wait_ge(pv2_done, len(TILES2))
                for t in range(MEM // P):
                    sc.dma_start(memtok[:, t, :], a["mem_2"][t * P:(t + 1) * P, :]).then_inc(mem_loaded, 16)

            def mem_turn():
                for k in range(KD):
                    sc.wait_ge(mem_turned, k + 1)
                    sc.activation(memT[:, k, :], ps[:, 6 + k % 2, 0:MEM], ACT.Copy).then_inc(mem_ready, 1)

            def evac_kv(d):
                r = d - D_KV
                sc.wait_ge(pe_seg, 2 * d + 2)
                if r < 2:
                    ins = sc.activation(mk[:, 2 * r:2 * r + 2, :], banks(d)[:, :, 0:MEM], ACT.Copy)
                elif r < 4:
                    ins = sc.activation(mv[:, :, UC * (r - 2):UC * (r - 1)], banks(d)[:, :, 0:UC], ACT.Copy)
                else:
                    ins = sc.activation(qm[:, 2 * (r - 4):2 * (r - 3), :], banks(d), ACT.Copy)
                ins.then_inc(banks_read[d % 2], 1)

            def merge():
                for c in range(KD):
                    sc.wait_ge(merged_ready, 16 + c + 1)
                    sc.wait_ge(pe_seg, 2 * D_OUT2)
                    sc.activation(hH[:, c, :], merged[:, c, :], ACT.Copy).then_inc(m_hi, 1)

            walk({"start": start, "split": split, "norm": norm, "apply": apply, "evac_in": evac_in, "turn": turn,
                  "pool": pool_step, "front": front, "mid": mid, "combine": combine, "evac_y": evac_y, "up": up,
                  "bias_rows": bias_rows, "evac_in2": evac_in2, "bias_load": bias_load, "evac_br": evac_br,
                  "front2": front2, "mid2": mid2, "back2": back2, "mem_load": mem_load, "mem_turn": mem_turn,
                  "evac_kv": evac_kv, "merge": merge})

        @block.vector
        def _(ve):
            own = [0]

            def link(ins):
                own[0] += 1
                ins.then_inc(dve_own, 1)
                ve.wait_ge(dve_own, own[0])

            def start():
                ve.memset(ones[:], 1.0).then_inc(ones_ready, 1)
                for t, r in enumerate(TABLE_ROWS):
                    if t == 0:
                        ve.wait_ge(vec_turned, 1)
                    ve.tensor_copy(vec[:, t, 0:r], ps[:, 4, t * P:t * P + r]).then_inc(vec_ready, 1)
                ve.wait_ge(vec_ready, 4)
                ve.wait_ge(k_loaded, 16)
                ve.wait_ge(silu_exp, 1)
                link(ve.tensor_scalar(small[:, 8:16], small[:, 0:8], 1.0, None, ALU.add))
                link(ve.reciprocal(small[:, 24:32], small[:, 8:16]))
                ve.tensor_tensor(small[:, 32:40], small[:, 24:32], v("c", 0, 8), ALU.mult).then_inc(cact_ready, 1)
                link(ve.tensor_tensor(small[:, 16:18], v("b_pool", 0, 2), v("pool_scale", 0, 2), ALU.mult))
                ve.wait_ge(pos_loaded, 16)
                link(ve.tensor_copy(posf[:], posi[:]))
                nb = GROUPS * TT
                link(ve.tensor_tensor(trig[:, 0, :, :], posf[:].unsqueeze(2).broadcast_to([P, nb, 8]),
                                      K[:, C_FREQ:C_FREQ + 8].unsqueeze(1).broadcast_to([P, nb, 8]), ALU.mult))
                c1 = 6.28125
                c2 = float(int((TWO_PI - c1) * 2 ** 20)) / 2 ** 20
                c3 = TWO_PI - c1 - c2
                for out_row, turns in ((2, 0.0), (3, 0.25)):
                    link(ve.tensor_scalar(trig[:, 1, :, :], trig[:, 0, :, :], 1.0 / TWO_PI, turns, ALU.mult, ALU.add))
                    link(ve.tensor_scalar(trig[:, 1, :, :], trig[:, 1, :, :], MAGIC, None, ALU.add))
                    link(ve.tensor_scalar(trig[:, 1, :, :], trig[:, 1, :, :], -MAGIC, None, ALU.add))
                    prev = trig[:, 0, :, :]
                    for c in (c1, c2, c3):
                        link(ve.scalar_tensor_tensor(out=trig[:, 4, :, :], in0=trig[:, 1, :, :], scalar=-c,
                                                     in1=prev, op0=ALU.mult, op1=ALU.add))
                        prev = trig[:, 4, :, :]
                    link(ve.tensor_scalar(trig[:, 4, :, :], trig[:, 4, :, :], turns * TWO_PI, 3.1415925, ALU.add, ALU.min))
                    ve.tensor_scalar(trig[:, out_row, :, :], trig[:, 4, :, :], -3.1415925, None, ALU.max
                                     ).then_inc(angle_ready, 1)
                for k in range(KD):
                    ve.wait_ge(x_turned, k + 1)
                    ve.tensor_copy(xT[:, k, :], ps[:, k % 4, :]).then_inc(x_ready, 1)
                ve.wait_ge(x_ready, KD)
                for i, count in enumerate((gate_conv, val_conv, hid_ready, hid_lo)):
                    for m in range(2):
                        ve.memset(act[:, m, i:i + 1], 0.0).then_inc(count, 1)

            def ada(part):
                ve.wait_ge(ada_used, ADA_FIRST if part == 0 else ADA_FIRST + ADA_REST)
                c0, c1 = (0, 16) if part == 0 else (16, 48)
                link(ve.tensor_tensor(mod[:, c0:c1], ps[:, 7, c0:c1], v("b_ada", c0, c1 - c0), ALU.add))
                if part == 0:
                    ve.scalar_tensor_tensor(out=colA[:, 0, :], in0=mod[:, 8:16], scalar=1.0, in1=v("g_pre_mix", 0, 8),
                                            op0=ALU.add, op1=ALU.mult).then_inc(mod_ready, 1)
                    ve.wait_ge(mod_ready, 1)
                else:
                    ve.tensor_tensor(colA[:, 1, :], mod[:, 16:24], v("g_post_mix", 0, 8), ALU.mult).then_inc(mod_ready, 1)
                    ve.scalar_tensor_tensor(out=colA[:, 2, :], in0=mod[:, 32:40], scalar=1.0, in1=v("g_pre_ffn", 0, 8),
                                            op0=ALU.add, op1=ALU.mult).then_inc(mod_ready, 1)
                    ve.tensor_tensor(colA[:, 3, :], mod[:, 40:48], v("g_post_ffn", 0, 8), ALU.mult).then_inc(mod_ready, 1)
                    ve.wait_ge(mod_ready, 4)

            def norm(n):
                w = norm_source[n][1]
                ve.wait_ge(ss_added, KD * n + KD)
                ve.tensor_scalar(nt[:, 0, 0:w], ps[:, 5, 0:w], 1.0 / D, EPS, ALU.mult, ALU.add).then_inc(var_ready, 1)
                ve.wait_ge(std_ready, n + 1)
                ve.reciprocal(ps[:, 4, 0:w], nt[:, 1, 0:w]).then_inc(rstd_ready, 1)
                ve.wait_ge(rstd_ready, n + 1)

            def apply(n):
                src, w = norm_source[n]
                hi, lo = (memH, memL) if n == N_MEM else (hH, hL)
                for k in range(KD + 1):
                    m = KD * SPLITS[n] + k
                    if k < KD:
                        if k >= 2:
                            ve.wait_ge(h_lo, m - 1)
                        ve.scalar_tensor_tensor(out=nt[:, k % 2, 0:w], in0=src[:, k, :], scalar=gains[n][:, k:k + 1],
                                                in1=ps[:, 4, 0:w], op0=ALU.mult, op1=ALU.mult).then_inc(scaled, 1)
                    if k >= 1:
                        ve.wait_ge(h_hi, m)
                        t = nt[:, (k - 1) % 2, 0:w]
                        h = hi[:, k - 1, :].bitcast(F32)
                        if n in shifts:
                            ins = ve.scalar_tensor_tensor(out=lo[:, k - 1, :], in0=t, scalar=shifts[n][:, k - 1:k],
                                                          in1=h, op0=ALU.add, op1=ALU.subtract)
                        else:
                            ins = ve.tensor_tensor(lo[:, k - 1, :], t, h, ALU.subtract)
                        ins.then_inc(h_lo, 1)

            def resid(n):
                src, w = norm_source[n]
                for k in range(KD):
                    m = KD * RESID[n] + k
                    if k >= 2:
                        ve.wait_ge(x_added, m - 1)
                    ve.scalar_tensor_tensor(out=nt[:, k % 2, :], in0=src[:, k, :], scalar=gains[n][:, k:k + 1],
                                            in1=ps[:, 4, :], op0=ALU.mult, op1=ALU.mult).then_inc(delta_ready, 1)

            def evac_in(d):
                if d == 0:
                    ve.memset(u[:, :, 0:POOL_PAD], 0.0).then_inc(pads_zero, 1)

            def turn(e):
                g, part = e // 2, e % 2
                d = 1 + 3 * g + part
                ve.wait_ge(banks_read[pair_of(d)], bank_use(d) + 1)
                ve.wait_ge(trig_ready, 2)
                q = qtok[:, e % 2, :, :].rearrange("p t (h f) -> p t h f", h=GH)
                t1, t2 = q[:, :, :, 0:8], q[:, :, :, 8:16]
                cos = cosT[:, g, :, :].unsqueeze(2).broadcast_to([P, TT, GH, 8])
                sin = sinT[:, g, :, :].unsqueeze(2).broadcast_to([P, TT, GH, 8])
                if e:
                    ve.wait_ge(rope_done, 2 * e)
                for i, (x, y) in enumerate(((t1, cos), (t2, sin), (t2, cos), (t1, sin))):
                    ins = ve.tensor_tensor(rope[:, i, :, :, :], x, y, ALU.mult)
                link(ins)
                ve.tensor_tensor(t1, rope[:, 0, :, :, :], rope[:, 1, :, :, :], ALU.subtract).then_inc(rope_done, 1)
                ve.tensor_tensor(t2, rope[:, 2, :, :, :], rope[:, 3, :, :, :], ALU.add).then_inc(rope_done, 1)

            def pool_step():
                ve.wait_ge(banks_read[0], 1)
                end = POOL_PAD + S
                for m in range(2):
                    A, B = win[:, 0, :], win[:, 1, :]
                    link(ve.tensor_tensor(A[:, 1:end], u[:, m, 1:end], u[:, m, 0:end - 1], ALU.add))
                    link(ve.tensor_tensor(B[:, 3:end], A[:, 3:end], A[:, 1:end - 2], ALU.add))
                    if m == 1:
                        link(ve.tensor_tensor(A[:, 7:end], B[:, 7:end], B[:, 3:end - 4], ALU.add))
                        link(ve.tensor_tensor(B[:, 15:end], A[:, 15:end], A[:, 7:end - 8], ALU.add))
                    for half, t in ((0, A), (1, B)):
                        r = slice(64 * half, 64 * half + 64)
                        rc = K[r, C_RC + 16 * m:C_RC + 16 * m + 16]
                        link(ve.tensor_tensor(t[r, 16:32], t[r, 16:32], rc, ALU.mult))
                        ve.tensor_tensor(u[r, m, 16:32], t[r, 16:32], u[r, m, 16:32], ALU.subtract).then_inc(pool_mixed, 1)
                        ve.scalar_tensor_tensor(out=u[r, m, 32:end], in0=t[r, 32:end], scalar=K[r, C_RW + m:C_RW + m + 1],
                                                in1=u[r, m, 32:end], op0=ALU.mult, op1=ALU.subtract).then_inc(pool_mixed, 1)
                    ve.wait_ge(pool_mixed, 4 * m + 4)
                for m in range(2):
                    ve.wait_ge(cat_hi, m + 1)
                    ve.tensor_tensor(hL[:, m, :], win[:, m, 0:S], hH[:, m, :].bitcast(F32), ALU.subtract).then_inc(cat_lo, 1)

            def front(n):
                g, b, nk = TILES1[n]
                w = P * nk
                ve.wait_ge(s_done, n + 1)
                if n >= 2:
                    ve.wait_ge(pt_done, key_blocks(n - 1))
                mask = K[:, C_PREV:C_PREV + w] if nk == 2 else (
                    K[:, C_BLOCK:C_BLOCK + P] if g == 2 else K[:, C_CAUSAL:C_CAUSAL + P])
                src = ps[:, 4:6, :].rearrange("p e (q w) -> p e q w", q=2)[:, :, :, 0:w]
                dst = S1[:, n % 2, :, :, 0:w]
                ve.tensor_tensor(dst, src, mask.unsqueeze(1).unsqueeze(1).broadcast_to([P, 2, 2, w]), ALU.add
                                 ).then_inc(s_read, 1)
                ve.wait_ge(s_read, n + 1)
                link(ve.tensor_reduce(md[:, n, 0, :].rearrange("p (e q) -> p e q", e=2), dst, X, ALU.max))
                ve.tensor_scalar(negm[:, n, :], md[:, n, 0, :], -DH ** -0.5, None, ALU.mult).then_inc(negm_ready, 1)

            def back(n):
                g, b, _ = TILES1[n]
                ve.wait_ge(pv_done, n + 1)
                src = ps[:, 7, 0:2 * P].rearrange("p (q t) -> p q t", q=2)
                st = ps[0:GH, 7, 2 * P:4 * P].rearrange("p (q t) -> p q t", q=2)
                o = oT[:, 2 * g:2 * g + 2, :]
                s = stats[:, :, g, :]
                if g == 0:
                    o, s = o[:, :, b * P:(b + 1) * P], s[:, :, b * P:(b + 1) * P]
                else:
                    o = o.rearrange("p c (i r) -> p c r i", r=TT)[:, :, b, :]
                    s = s.rearrange("p c (i r) -> p c r i", r=TT)[:, :, b, :]
                ve.tensor_copy(o, src).then_inc(pv_read, 1)
                ve.tensor_copy(s, st).then_inc(pv_read, 1)

            def combine():
                ve.wait_ge(pv_read, 2 * len(TILES1))
                link(ve.tensor_tensor(amax[:, 0, :], stats[:, 0, 0, :], stats[:, 0, 1, :], ALU.max))
                link(ve.tensor_tensor(amax[:, 0, :], amax[:, 0, :], stats[:, 0, 2, :], ALU.max))
                wide = [GH, GROUPS, S]
                ve.tensor_tensor(alpha[:], stats[:, 0, :, :], amax[:, 0, :].unsqueeze(1).broadcast_to(wide), ALU.subtract
                                 ).then_inc(gap_ready, 1)
                ve.wait_ge(gap_exp, 1)
                link(ve.tensor_tensor(stats[:, 1, :, :], stats[:, 1, :, :], alpha[:], ALU.mult))
                link(ve.tensor_tensor(amax[:, 0, :], stats[:, 1, 0, :], stats[:, 1, 1, :], ALU.add))
                link(ve.tensor_tensor(amax[:, 0, :], amax[:, 0, :], stats[:, 1, 2, :], ALU.add))
                link(ve.reciprocal(amax[:, 1, :], amax[:, 0, :]))
                ve.tensor_tensor(alpha[:], alpha[:], amax[:, 1, :].unsqueeze(1).broadcast_to(wide), ALU.mult
                                 ).then_inc(alpha_ready, 1)
                for hp in range(2):
                    ve.wait_ge(alpha_spread, hp + 1)
                    if hp:
                        ve.wait_ge(cat_lo, 3)
                    for g in range(GROUPS):
                        ins = ve.tensor_tensor(comb[:, g, :], oT[:, 2 * g + hp, :], ps[:, 4 * (1 - hp) + g, :], ALU.mult)
                    link(ins)
                    link(ve.tensor_tensor(comb[:, 0, :], comb[:, 0, :], comb[:, 1, :], ALU.add))
                    ve.tensor_tensor(comb[:, 0, :], comb[:, 0, :], comb[:, 2, :], ALU.add).then_inc(attn_ready, 1)
                    ve.wait_ge(attn_ready, hp + 1)
                    ve.wait_ge(cat_hi, 3 + hp)
                    ve.tensor_tensor(hL[:, 2 + hp, :], comb[:, 0, :], hH[:, 2 + hp, :].bitcast(F32), ALU.subtract
                                     ).then_inc(cat_lo, 1)

            def up(f):
                d0 = (D_UP1, D_UP2)[f]
                done = 2 * FF_PAIRS * f
                own0 = own[0]
                per = 2 + 2 * f
                with ve.Fori(0, FF_PAIRS) as j:
                    n = [0]

                    def conv(m, half):
                        t, z = act[:, 2 * half + m, :], ps[:, 2 * half + m, :]
                        if f == 0:
                            w1, w0 = v("conv_w", j * 2 + (22 + m)), v("conv_w", j * 2 + m)
                            ve.wait_ge(seeded, j * 2 + (m + 1))
                        else:
                            w1, w0 = v("ffn_conv_w_2", j * 2 + (44 + 22 * half + m)), v("ffn_conv_w_2", j * 2 + (22 * half + m))
                            ve.wait_ge(seeded, j * 4 + (2 * FF_PAIRS + 2 * half + m + 1))
                        n[0] += 1
                        ve.scalar_tensor_tensor(out=t[:, 1:S], in0=z[:, 0:S - 1], scalar=w1, in1=t[:, 1:S],
                                                op0=ALU.mult, op1=ALU.add).then_inc(dve_own, 1)
                        ve.wait_ge(dve_own, j * per + (own0 + n[0]))
                        return ve.scalar_tensor_tensor(out=t[:, 2:S], in0=z[:, 0:S - 2], scalar=w0, in1=t[:, 2:S],
                                                       op0=ALU.mult, op1=ALU.add)

                    conv(0, 0).then_inc(gate_conv, 1)
                    conv(1, 0).then_inc(gate_conv, 1)
                    if f == 1:
                        conv(0, 1).then_inc(val_conv, 1)
                        conv(1, 1).then_inc(val_conv, 1)
                        ve.wait_ge(val_conv, j * 2 + 4)
                    for m in range(2):
                        ve.wait_ge(gelu_done, j * 2 + (m + 1 + done))
                        if f == 0:
                            ve.wait_ge(pe_seg, j * 4 + 2 * d0 + 3 + m)
                            other = ps[:, 2 + m, :]
                        else:
                            other = act[:, 2 + m, :]
                        ve.tensor_tensor(act[:, m, :], act[:, m, :], other, ALU.mult).then_inc(hid_ready, 1)
                    for m in range(2):
                        ve.wait_ge(hid_hi, j * 2 + (m + 1 + done))
                        ve.tensor_tensor(hidL[:, bass.ds(j * 2 + m, 1), :], act[:, m:m + 1, :],
                                         hidH[:, bass.ds(j * 2 + m, 1), :].bitcast(F32), ALU.subtract).then_inc(hid_lo, 1)
                    assert n[0] == per
                own[0] += per * FF_PAIRS

            def bias_rows():
                ve.wait_ge(rel_done, 1)
                ve.tensor_tensor(rrow[:, 0:S], ps[0:HEADS2, 6, :], hot[0:HEADS2, REL:REL + S], ALU.add).then_inc(rrow_ready, 1)
                ve.tensor_tensor(rrow[:, S:REL], ps[0:HEADS2, 7, 0:P], hot[0:HEADS2, REL + S:2 * REL], ALU.add
                                 ).then_inc(rrow_ready, 1)

            def evac_in2(d):
                r = d - D_IN2
                kind, j = r // 2, r % 2
                if kind == 0 and j == 0:
                    ve.wait_ge(rrow_stored, 16)
                    ve.memset(cc[:, :, 0:2], 0.0).then_inc(pads_zero, 1)
                elif kind == 1:
                    ve.wait_ge(pe_seg, 2 * d + 2)
                    ve.wait_ge(banks_read[j], bank_use(d - 2) + 1)
                    t = cc[:, 2 * j:2 * j + 2, 2:]
                    ve.tensor_tensor(t, t, banks(d), ALU.mult).then_inc(banks_read[j], 1)
                elif kind == 2:
                    ve.wait_ge(banks_read[j], bank_use(d))
                    ve.wait_ge(pads_zero, 2)
                    for m in range(2):
                        c = 2 * j + m
                        link(ve.tensor_scalar(nt[:, m, :], cc[:, c, 2:2 + S], v("conv_mix_w_2", 8 + c), None, ALU.mult))
                        for tap in (1, 0):
                            link(ve.scalar_tensor_tensor(out=nt[:, m, :], in0=cc[:, c, tap:tap + S],
                                                         scalar=v("conv_mix_w_2", 4 * tap + c), in1=nt[:, m, :],
                                                         op0=ALU.mult, op1=ALU.add))
                    ve.wait_ge(pe_seg, 2 * d + 2)
                    for m in range(2):
                        c = 2 * j + m
                        if j == 1:
                            ve.wait_ge(conv_lo, c - 1)
                        ve.tensor_tensor(sq[:, m, :], nt[:, m, :], ps[:, 2 * pair_of(d) + m, :], ALU.mult
                                         ).then_inc(banks_read[j] if m else conv_y, 1)
                    for m in range(2):
                        c = 2 * j + m
                        ve.wait_ge(conv_hi, c + 1)
                        ve.tensor_tensor(bufAL[:, c, :], sq[:, m, :], bufAH[:, c, :].bitcast(F32), ALU.subtract
                                         ).then_inc(conv_lo, 1)

            def evac_br(d):
                br = next(i for i, d0 in ((2, D_BR2), (1, D_BR1), (0, D_BR0)) if d >= d0)
                j, r = (d - (D_BR0, D_BR1, D_BR2)[br]) // 2, (d - D_BR0) % 2
                if not r:
                    return
                g = d - 1
                ve.wait_ge(banks_read[pair_of(g)], bank_use(g) + 1)
                for m in range(2):
                    c = 2 * j + m
                    ve.wait_ge(pe_seg, 2 * d + 1 + m)
                    z = ps[:, 2 * pair_of(d) + m, :]
                    ins = ve.tensor_tensor(sg[:, m, :], sg[:, m, :], z, ALU.mult)
                    if m == 0:
                        link(ins)
                    else:
                        ins.then_inc(banks_read[pair_of(d)], 1)
                        ve.wait_ge(banks_read[pair_of(d)], bank_use(d) + 1)
                    if br == 0:
                        ve.tensor_copy(merged[:, c, :], sg[:, m, :]).then_inc(merged_ready, 1)
                    else:
                        ve.tensor_tensor(merged[:, c, :], merged[:, c, :], sg[:, m, :], ALU.add).then_inc(merged_ready, 1)

            def front2(n):
                kind, i, h, nb, _, _ = tile2(n)
                w = P * nb
                ve.wait_ge(s2_done, n + 1)
                if n >= 2:
                    ve.wait_ge(pt2_done, n - 1)
                if kind == "self":
                    if n == 0:
                        ve.wait_ge(bias_loaded, 32)
                    bias = (W0 if h < 4 else W1)[:, h % 4, S - w:S]
                    ve.scalar_tensor_tensor(out=S2[:, n % 2, 0:w], in0=ps[:, 4 + n % 2, 0:w], scalar=DH ** -0.5, in1=bias,
                                            op0=ALU.mult, op1=ALU.add).then_inc(s2_read, 1)
                    ve.wait_ge(s2_read, n + 1)
                    ve.tensor_reduce(md2[:, 0, n:n + 1], S2[:, n % 2, 0:w], X, ALU.max, negate=True).then_inc(negm2_ready, 1)
                else:
                    link(ve.tensor_reduce(md2[:, 2, n:n + 1], ps[:, 4 + n % 2, 0:w], X, ALU.max))
                    ve.tensor_scalar(md2[:, 0, n:n + 1], md2[:, 2, n:n + 1], -P ** -0.5, None, ALU.mult
                                     ).then_inc(negm2_ready, 1)

            def mid2(n):
                w = P * tile2(n)[3]
                ve.wait_ge(exp2_done, n + 1)
                link(ve.reciprocal(md2[:, 2, n:n + 1], md2[:, 1, n:n + 1]))
                ve.tensor_scalar(S2[:, n % 2, 0:w], S2[:, n % 2, 0:w], md2[:, 2, n:n + 1], None, ALU.mult
                                 ).then_inc(p2_scaled, 1)

            def back2(n):
                kind, i, h, _, c, row = tile2(n)
                if kind == "self" and row == 0:
                    return
                hi, lo = (bufBH, bufBL) if kind == "self" else (bufAH, bufAL)
                q = slice(i * P, (i + 1) * P)
                ve.wait_ge(o2_hi, pairs_before(n) + 1)
                ve.tensor_tensor(lo[:, c, q], ps[:, 7, 0:P], hi[:, c, q].bitcast(F32), ALU.subtract).then_inc(o2_lo, 1)

            def merge():
                for c in range(KD):
                    ve.wait_ge(m_hi, c + 1)
                    ve.tensor_tensor(hL[:, c, :], merged[:, c, :], hH[:, c, :].bitcast(F32), ALU.subtract).then_inc(m_lo, 1)

            def finish():
                for t in range(TT):
                    ve.wait_ge(out_turned, t + 1)
                    src = ps[:, 2 * (t % 2):2 * (t % 2) + 2, :]
                    ve.tensor_copy(otok[:, t, :].rearrange("p (b n) -> p b n", b=2), src).then_inc(out_copied, 1)

            walk({"start": start, "ada": ada, "norm": norm, "apply": apply, "resid": resid, "evac_in": evac_in,
                  "turn": turn, "pool": pool_step, "front": front, "back": back, "combine": combine, "up": up,
                  "bias_rows": bias_rows, "evac_in2": evac_in2, "evac_br": evac_br, "front2": front2, "mid2": mid2,
                  "back2": back2, "merge": merge, "finish": finish})

        @block.tensor
        def _(pe):
            def start():
                pe.wait_ge(k_loaded, 16)
                pe.wait_ge(vec_loaded, 16 * len(VEC))
                for t, r in enumerate(TABLE_ROWS):
                    mm = pe.transpose(ps[:, 4, t * P:t * P + r], vrow[0:r, t, :], K[0:r, C_ID:C_ID + r])
                mm.then_inc(vec_turned, 1)
                pe.wait_ge(x_loaded, 16 * TT)
                for k in range(KD):
                    if k >= 4:
                        pe.wait_ge(x_ready, k - 3)
                    for t in range(TT):
                        mm = pe.transpose(ps[:, k % 4, t * P:(t + 1) * P], xtok[:, t, k * P:(k + 1) * P], ident)
                    mm.then_inc(x_turned, 1)

            def ada(part):
                first, count = (0, ADA_FIRST) if part == 0 else (ADA_FIRST, ADA_REST)
                r0 = 0 if part == 0 else raw_index(D_OUT - 1) + 1
                if part == 0:
                    pe.wait_ge(cact_ready, 1)
                else:
                    pe.wait_ge(turn_read, 12)
                for i in range(count):
                    r = r0 + i
                    pe.wait_ge(raw_loaded[r % 2], 16 * (r // 2 + 1))
                    for m in range(2):
                        n = 2 * (first + i) + m
                        for k in range(KD):
                            mm = pe.matmul(ps[:, 7, n:n + 1], raw[:, r % 2, k, m * P:(m + 1) * P],
                                           small[:, 32 + k:33 + k], start=(k == 0), stop=(k == KD - 1))
                    mm.then_inc(ada_used, 1)

            def norm(n):
                w = norm_source[n][1]
                if n == 0:
                    pe.wait_ge(ones_ready, 1)
                for k in range(KD):
                    if k == 0 and n:
                        pe.wait_ge(var_ready, n)
                    pe.wait_ge(sq_ready, KD * n + k + 1)
                    pe.matmul(ps[:, 5, 0:w], ones[:], sq[:, k % 2, 0:w], start=(k == 0), stop=(k == KD - 1)
                              ).then_inc(ss_added, 1)

            def product(out, lhs, rhs, first, last):
                for i, (x, y) in enumerate(((0, 0), (0, 1), (1, 0))):
                    mm = pe.matmul(out, lhs[x], rhs[y], start=(first and i == 0), stop=(last and i == 2))
                return mm

            def source_of(d):
                if d < D_OUT:
                    return (hH, hL), 0
                if d < D_UP1:
                    return (hH, hL), None
                if D_DOWN1 <= d < D_IN2 or d >= D_DOWN2:
                    return (hidH, hidL), None
                for d0, buf in ((D_BR0, (bufAH, bufAL)), (D_BR1, (bufBH, bufBL)), (D_BR2, (bufAH, bufAL))):
                    if d0 <= d < d0 + 8 and (d - d0) % 2:
                        return buf, None
                if D_KV <= d < D_KV + 4:
                    return (memH, memL), None
                return (hH, hL), None

            first_of = {D_IN: N_PRE1, D_IN2: N_PRE2, D_KV: N_MEM}

            def seg(d, m):
                p = pair_of(d)
                down = D_DOWN1 <= d < D_IN2 or d >= D_DOWN2
                q = ((d - D_DOWN1) % 4 if d < D_IN2 else (d - D_DOWN2) % 4) if down else 0
                if m == 0:
                    pe.wait_ge(lo_done, d + 1)
                    if q == 0 and bank_use(d) > 0:
                        pe.wait_ge(banks_read[p], bank_use(d))
                    if d == D_OUT:
                        pe.wait_ge(cat_lo, 4)
                    if d in (D_DOWN1, D_DOWN2):
                        pe.wait_ge(hid_lo, 2 + (1 if d == D_DOWN1 else 2) * 2 * FF_PAIRS)
                    if d == D_BR0 + 1:
                        pe.wait_ge(conv_lo, 4)
                    if d == D_BR1 + 1:
                        pe.wait_ge(o2_lo, pairs_before(len(TILES2)))
                    if d == D_BR2 + 1:
                        pe.wait_ge(o2_lo, pairs_before(len(TILES23)))
                    if d == D_OUT2:
                        pe.wait_ge(m_lo, KD)
                src, _ = source_of(d)
                _, nk = unit_source(d)
                k0 = DOWN_K0[q] if down else 0
                s = d % 2
                by_token = (D_IN < d < D_OUT) or (D_IN2 + 10 <= d < D_BR0) or d in (D_KV + 2, D_KV + 3)
                if not by_token:
                    w = MEM if D_KV <= d < D_KV + 4 else S
                    for k in range(nk):
                        if d in first_of and m == 0:
                            pe.wait_ge(h_lo, KD * SPLITS[first_of[d]] + k + 1)
                        cols = slice(m * P, (m + 1) * P)
                        mm = product(ps[:, 2 * p + m, 0:w], (WH[:, s, k, cols], WL[:, s, k, cols]),
                                     (src[0][:, k0 + k, :], src[1][:, k0 + k, :]),
                                     k == 0 and q == 0, k == nk - 1 and (not down or q == 3))
                else:
                    g = (d - 1) // 3 if d < D_OUT else 0
                    tiles = (m,) if d >= D_KV else (2 * m, 2 * m + 1)
                    for t in tiles:
                        o = ps[:, 2 * p + m, t % 2 * UC:t % 2 * UC + UC] if d < D_KV else ps[:, 2 * p + m, 0:UC]
                        for k in range(nk):
                            mm = product(o, (tokens(src[0], k, g, t), tokens(src[1], k, g, t)),
                                         (WH[:, s, k, :], WL[:, s, k, :]), k == 0, k == nk - 1)
                mm.then_inc(pe_seg, 1)

            def turn(e):
                pe.wait_ge(rope_done, 2 * e + 2)
                for hp in range(2):
                    if e:
                        pe.wait_ge(turn_read, 2 * (e - 1) + hp + 1)
                    for t in range(TT):
                        mm = pe.transpose(ps[:, 6 + hp, t * P:(t + 1) * P], qtok[:, e % 2, t, hp * P:(hp + 1) * P], ident)
                    mm.then_inc(turned, 1)

            def pool_step():
                pe.wait_ge(wpool_loaded, 16)
                pe.wait_ge(banks_read[0], 5)
                pe.wait_ge(banks_read[1], 5)
                pe.wait_ge(pool_mixed, 8)
                for m in range(2):
                    for half in range(2):
                        r = slice(64 * half, 64 * half + 64)
                        mm = pe.matmul(ps[r, 2 * m + half, :], wpool[r, m, :], u[r, m, POOL_PAD:], start=True, stop=True)
                    mm.then_inc(pool_done, 1)

            def front(n):
                g, b, nk = TILES1[n]
                pe.wait_ge(turn_read, 4 * g + 4)
                if n:
                    pe.wait_ge(s_read, n)
                else:
                    pe.wait_ge(h_lo, KD)
                k0 = P * (b - 1) if nk == 2 else P * b
                for q in range(2):
                    for e in range(2):
                        r = slice(64 * e, 64 * e + 64)
                        mm = pe.matmul(ps[:, 4 + e, 256 * q:256 * q + P * nk], qT[r, 2 * g + q, P * b:P * b + P],
                                       kT[r, 2 * g + q, k0:k0 + P * nk], start=True, stop=True)
                mm.then_inc(s_done, 1)

            def mid(n):
                pe.wait_ge(exp_done, GH * (n + 1))
                for kb in range(TILES1[n][2]):
                    i = key_blocks(n) + kb
                    if i:
                        pe.wait_ge(pt_read, i)
                    for x in range(GH):
                        mm = pe.transpose(ps[:, 6, P * x:P * x + P],
                                          S1[:, n % 2, x // 2, x % 2, P * kb:P * kb + P], ident)
                    mm.then_inc(pt_done, 1)

            def back(n):
                g, b, nk = TILES1[n]
                pe.wait_ge(pt_read, key_blocks(n + 1))
                if n:
                    pe.wait_ge(pv_read, 2 * n)
                else:
                    pe.wait_ge(mod_ready, 4)
                pe.wait_ge(banks_read[pair_of(3 + 3 * g)], bank_use(3 + 3 * g) + 1)
                for q in range(2):
                    for e in range(2):
                        h = 2 * q + e
                        for kb in range(nk):
                            pe.matmul(ps[64 * e:64 * e + 64, 7, P * q:P * q + P],
                                      V1[:, b - nk + 1 + kb, g, DH * h:DH * h + DH],
                                      PT1[:, n % 2, kb, P * (2 * e + q):P * (2 * e + q) + P],
                                      start=(kb == 0), stop=(kb == nk - 1))
                for i in range(2):
                    mm = pe.transpose(ps[0:GH, 7, P * (2 + i):P * (3 + i)], md[:, n, i, :], ident)
                mm.then_inc(pv_done, 1)

            def combine():
                pe.wait_ge(alpha_ready, 1)
                pe.wait_ge(pool_val, 4)
                for hp in range(2):
                    for g in range(GROUPS):
                        mm = pe.matmul(ps[:, 4 * (1 - hp) + g, :], K[0:GH, C_SEL + P * hp:C_SEL + P * hp + P],
                                       alpha[:, g, :], start=True, stop=True)
                    mm.then_inc(alpha_spread, 1)

            def up(f):
                d0 = (D_UP1, D_UP2)[f]
                done = 2 * FF_PAIRS * f
                pe.wait_ge(h_lo, KD * SPLITS[(N_PREF1, N_PREF2)[f]] + KD)
                pe.wait_ge(banks_read[0], bank_use(d0))
                pe.wait_ge(banks_read[1], bank_use(d0))
                with pe.Fori(0, FF_PAIRS) as j:
                    for half in range(2):
                        pe.wait_ge(lo_done, j * 2 + (d0 + half + 1))
                        if half == 0:
                            pe.wait_ge(gate_conv, j * 2 + (2 + done))
                        elif f == 0:
                            pe.wait_ge(hid_ready, j * 2 + 2)
                        else:
                            pe.wait_ge(val_conv, j * 2 + 2)
                        for m in range(2):
                            cols = slice(m * P, (m + 1) * P)
                            for k in range(KD):
                                mm = product(ps[:, 2 * half + m, :], (WH[:, half, k, cols], WL[:, half, k, cols]),
                                             (hH[:, k, :], hL[:, k, :]), k == 0, k == KD - 1)
                            mm.then_inc(pe_seg, 1)

            def bias_rows():
                pe.wait_ge(hot_loaded, 32)
                pe.matmul(ps[0:HEADS2, 6, :], rel[:], hot[:, 0:S], start=True, stop=True)
                pe.matmul(ps[0:HEADS2, 7, 0:P], rel[:], hot[:, S:REL], start=True, stop=True).then_inc(rel_done, 1)

            def front2(n):
                kind, i, h, nb, c, row = tile2(n)
                if n >= 2:
                    pe.wait_ge(exp2_done, n - 1)
                qs = slice(i * P, (i + 1) * P)
                if kind == "self":
                    if n == 0:
                        pe.wait_ge(banks_read[0], bank_use(D_BR0))
                        pe.wait_ge(banks_read[1], bank_use(D_BR0 + 1))
                    r = slice(row, row + DH)
                    mm = pe.matmul(ps[:, 4 + n % 2, 0:P * nb], q2[r, c, qs], k2[r, c, 0:P * nb], start=True, stop=True)
                else:
                    if n == len(TILES2):
                        pe.wait_ge(banks_read[0], bank_use(D_BR2))
                        pe.wait_ge(banks_read[1], bank_use(D_BR2 + 1))
                    mm = pe.matmul(ps[:, 4 + n % 2, 0:MEM], qm[:, c, qs], mk[:, c, :], start=True, stop=True)
                mm.then_inc(s2_done, 1)

            def mid2(n):
                nb = tile2(n)[3]
                pe.wait_ge(p2_scaled, n + 1)
                if n:
                    pe.wait_ge(pt2_read, n)
                for b in range(nb):
                    mm = pe.transpose(ps[:, 6, P * b:P * b + P], S2[:, n % 2, P * b:P * b + P], ident)
                mm.then_inc(pt2_done, 1)

            def back2(n):
                kind, i, h, nb, c, row = tile2(n)
                pe.wait_ge(pt2_read, n + 1)
                if pairs_before(n):
                    pe.wait_ge(o2_lo, pairs_before(n))
                for b in range(nb):
                    if kind == "self":
                        out, val = ps[row:row + DH, 7, 0:P], V2[:, b, DH * h:DH * h + DH]
                    else:
                        out, val = ps[:, 7, 0:P], mv[:, b, P * h:P * h + P]
                    mm = pe.matmul(out, val, PT2[:, n % 2, P * b:P * b + P], start=(b == 0), stop=(b == nb - 1))
                mm.then_inc(pv2_done, 1)

            def mem_turn():
                pe.wait_ge(mem_loaded, 16 * (MEM // P))
                for k in range(KD):
                    if k >= 2:
                        pe.wait_ge(mem_ready, k - 1)
                    for t in range(MEM // P):
                        mm = pe.transpose(ps[:, 6 + k % 2, t * P:(t + 1) * P], memtok[:, t, k * P:(k + 1) * P], ident)
                    mm.then_inc(mem_turned, 1)

            def finish():
                for t in range(TT):
                    if t >= 2:
                        pe.wait_ge(out_copied, t - 1)
                    pe.wait_ge(x_added, KD * 4)
                    for k in range(KD):
                        mm = pe.transpose(ps[:, 2 * (t % 2) + k // 4, k % 4 * P:(k % 4 + 1) * P],
                                          xT[:, k, t * P:(t + 1) * P], ident)
                    mm.then_inc(out_turned, 1)

            walk({"start": start, "ada": ada, "norm": norm, "seg": seg, "turn": turn, "pool": pool_step, "front": front,
                  "mid": mid, "back": back, "combine": combine, "up": up, "bias_rows": bias_rows, "front2": front2,
                  "mid2": mid2, "back2": back2, "mem_turn": mem_turn, "finish": finish})


def tables():
    import numpy as np

    t = np.zeros((P, C_END), np.float32)
    t[:, C_ID:C_ID + P] = np.eye(P)
    q, k = np.arange(P)[:, None], np.arange(P)[None, :]
    t[:, C_PREV:C_PREV + P] = np.where(k >= q, 0.0, NEG)
    t[:, C_CAUSAL:C_CAUSAL + P] = np.where(k <= q, 0.0, NEG)
    t[:, C_BLOCK:C_BLOCK + P] = np.where((k <= q) & (k % 4 == q % 4), 0.0, NEG)
    t[:, C_FREQ:C_FREQ + 8] = np.float32(500000.0) ** (-np.arange(0, 16, 2, dtype=np.float32) / np.float32(16))
    for x in range(GH):
        e, c = x // 2, x % 2
        t[x, C_SEL + P * c + 64 * e:C_SEL + P * c + 64 * e + 64] = 1.0
    for g, w in enumerate(WINDOWS):
        r = slice(64 * (g % 2), 64 * (g % 2) + 64)
        t[r, C_RC + 16 * (g // 2):C_RC + 16 * (g // 2) + 16] = 1.0 / np.minimum(np.arange(16) + 1.0, w)
        t[r, C_RW + g // 2] = 1.0 / w
    hot = np.zeros((BUCKETS, 2 * REL), np.float32)
    dist = np.arange(S)
    far = np.maximum(dist, BUCKETS // 2).astype(np.float32)
    large = BUCKETS // 2 + (np.log(far / np.float32(16)) / np.float32(np.log(64.0)) * np.float32(16)).astype(np.int32)
    bucket = np.where(dist < BUCKETS // 2, dist, np.minimum(large, BUCKETS - 1))
    hot[bucket[::-1], np.arange(S)] = 1.0
    hot[:, REL + S:] = NEG
    return t, hot


_ROWS = {"c": 8, "b_ada": 48, "g_pre_mix": 8, "g_post_mix": 8, "g_pre_ffn": 8, "g_post_ffn": 8, "b_pool": 2,
         "pool_scale": 2, "b_gate_2": 24, "conv_w": 66, "conv_b": 22, "g_pre_mix_2": 8, "g_post_mix_2": 8,
         "g_pre_ffn_2": 8, "g_post_ffn_2": 8, "g_mem_2": 8, "ffn_conv_w_2": 132, "conv_mix_w_2": 12,
         "ffn_conv_b_2": 44}
_SHAPES = {"x": (S, D), "positions": (S,), "w_ada": (D, 6 * D), "w_in": (D, 2560), "w_pool": (4, DH, DH),
           "w_out": (512, D), "w_up": (D, 2 * D_FF), "w_down": (D_FF, D), "mem_2": (MEM, D),
           "rel_bias_2": (BUCKETS, HEADS2), "w_in_2": (D, 6656), "w_conv_out_2": (512, D),
           "w_attn_out_2": (512, D), "w_mem_kv_2": (D, D), "w_mem_out_2": (512, D), "w_out_2": (D, D),
           "w_up_2": (D, 2 * D_FF), "w_down_2": (D_FF, D)}


def kernel(**inputs):
    import numpy as np
    import concourse.bacc as bacc
    from concourse.bass_utils import run_bass_kernel_spmd

    nc = bacc.Bacc("TRN2", target_bir_lowering=False, num_devices=1)
    arrays, aps = {}, {}
    shapes = dict(_SHAPES, **{n: (r, P) for n, r in _ROWS.items()})
    table, hot = tables()
    given = {n: np.ascontiguousarray(inputs[n]).reshape(shape) for n, shape in shapes.items()}
    given.update(table=table, hot=hot)
    pos = given["positions"]
    given["positions"] = np.concatenate([pos.reshape(TT, P).T, pos.reshape(P, TT), pos.reshape(P, TT)], axis=1)
    for name, x in given.items():
        arrays[name + "_dram"] = x
        aps[name] = nc.dram_tensor(name + "_dram", x.shape, mybir.dt.from_np(x.dtype), kind="ExternalInput").ap()
    out = nc.dram_tensor("out_dram", (S, D), F32, kind="ExternalOutput").ap()
    build(nc, aps, out)
    r = run_bass_kernel_spmd(nc, [arrays], core_ids=[0])
    return r.results[0]["out_dram"].reshape(1, S, D)
```

```python
from contextlib import ExitStack

import concourse.bass as bass
from concourse import mybir

F32 = mybir.dt.float32
F32R = mybir.dt.float32r
I32 = mybir.dt.int32
ACT = mybir.ActivationFunctionType
ALU = mybir.AluOpType
X = mybir.AxisListType.X

P = 128
D = 1024
S = 512
KD = D // P
TT = S // P
UC = 256
D_FF = 2816
KF = D_FF // P
FF_PAIRS = D_FF // UC
EPS = 1e-6
NEG = -1e30
DH = 64
GROUPS = 3
GH = 4
POOL_PAD = 16
WINDOWS = (2, 4, 8, 16)
HEADS2 = 8
MEM = 256
MEM_HEADS = 4
TWO_PI = 6.283185307179586
MAGIC = 12582912.0
BUCKETS = 32
REL = S + P

C_ID = 0
C_PREV, C_CAUSAL, C_BLOCK = 0, 128, 256
C_FREQ, C_SEL, C_RC, C_RW, C_END = 384, 392, 648, 680, 810

VEC = {
    "c": (0, 0, 8), "b_ada": (0, 8, 48), "g_pre_mix": (0, 56, 8), "g_post_mix": (0, 64, 8),
    "g_pre_ffn": (0, 72, 8), "g_post_ffn": (0, 80, 8), "b_pool": (0, 88, 2), "pool_scale": (0, 90, 2),
    "b_gate_2": (0, 92, 24),
    "conv_w": (1, 0, 66), "conv_b": (1, 66, 22), "g_pre_mix_2": (1, 88, 8), "g_post_mix_2": (1, 96, 8),
    "g_pre_ffn_2": (1, 104, 8), "g_post_ffn_2": (1, 112, 8), "g_mem_2": (1, 120, 8),
    "ffn_conv_w_2": (2, 0, 88), "conv_mix_w_2": (2, 88, 12),
    "ffn_conv_w_2b": (3, 0, 44), "ffn_conv_b_2": (3, 44, 44),
}
TABLE_ROWS = (116, 128, 100, 88)

D_IN, D_OUT, D_UP1, D_DOWN1 = 0, 10, 14, 36
D_IN2, D_BR0, D_KV, D_BR1, D_BR2 = 52, 64, 72, 78, 86
D_OUT2, D_UP2, D_DOWN2, D_END = 94, 98, 120, 136
ADA_FIRST, ADA_REST = 8, 16
DOWN_K = (6, 6, 5, 5)
DOWN_K0 = (0, 6, 12, 17)


def bank_use(d):
    if d <= D_UP1:
        return d // 2
    if d < D_IN2:
        return D_UP1 // 2 + (d - D_DOWN1) // 8
    if d <= D_UP2:
        return D_UP1 // 2 + 2 + (d - D_IN2) // 2
    return D_UP1 // 2 + 2 + (D_UP2 - D_IN2) // 2 + (d - D_DOWN2) // 8


def pair_of(d):
    if D_DOWN1 <= d < D_IN2:
        return (d - D_DOWN1) // 4 % 2
    if d >= D_DOWN2:
        return (d - D_DOWN2) // 4 % 2
    return d % 2


TILES1 = [(g, b, 2 if g == 0 and b > 0 else 1) for g in range(GROUPS) for b in range(TT)]
TILES2 = [("self", i, h, i + 1) for i in range(TT) for h in range(HEADS2)]
TILES3 = [("mem", i, h, MEM // P) for i in range(TT) for h in range(MEM_HEADS)]
TILES23 = TILES2 + TILES3

(N_PRE1, N_POST1, N_PREF1, N_POSTF1, N_PRE2, N_MEM, N_POST2, N_PREF2, N_POSTF2) = range(9)
SPLITS = {N_PRE1: 0, N_PREF1: 1, N_PRE2: 2, N_MEM: 3, N_PREF2: 4}
RESID = {N_POST1: 0, N_POSTF1: 1, N_POST2: 2, N_POSTF2: 3}


def build(nc, a, out):
    ctx = ExitStack()
    with ctx:
        def sb(name, shape, dt=F32):
            return ctx.enter_context(nc.sbuf_tensor(name, shape, dt))

        def sem(name):
            return ctx.enter_context(nc.semaphore(name))

        ident_t = sb("ident_t", [P, P])
        ones = sb("ones", [P, P])
        vec = sb("vec", [P, 4, P])
        mod = sb("mod", [P, 48])
        colA = sb("colA", [P, 4, KD])
        small = sb("small", [P, 64])
        xT = sb("xT", [P, KD, S])
        hH = sb("hH", [P, KD, S], F32R)
        hL = sb("hL", [P, KD, S], F32R)
        raw = sb("raw", [P, 2, KD, UC])
        WH = sb("WH", [P, 2, KD, UC], F32R)
        WL = sb("WL", [P, 2, KD, UC], F32R)
        base = (nc.sbuf_base + 31) // 32 * 32
        room = nc.sbuf_usable_end - base
        ctx.enter_context(nc.sbuf_tensor("arena", [P, (room - 64) // 4], F32))

        def at(name, shape, kib, dt=F32):
            free = 4
            for n in shape[1:]:
                free *= n
            assert kib * 1024 + free <= room - 64, (name, kib * 1024 + free, room)
            return nc.alloc_sbuf_tensor_at(name, shape, dt, offset=base + int(kib * 1024))

        sq = at("sq", [P, 2, S], 104.1875)
        nt = at("nt", [P, 2, S], 4)
        dl = at("dl", [P, 4, S], 8)
        vrow = at("vrow", [P, 4, P], 8)
        xtok = at("xtok", [P, TT, D], 12)
        posi = at("posi", [P, GROUPS * TT], 30, I32)
        posf = at("posf", [P, GROUPS * TT], 30.5)
        trig = at("trig", [P, 5, GROUPS * TT, 8], 31)
        u = at("u", [P, 2, POOL_PAD + S], 8)
        win = at("win", [P, 2, POOL_PAD + S], 12.5)
        qtok = at("qtok", [P, 2, TT, UC], 17)
        rope = at("rope", [P, 4, TT, GH, 8], 25)
        wpool = at("wpool", [P, 2, DH], 28)
        K = at("K", [P, C_END - P], 99.5)
        adaw = at("adaw", [P, 3, KD, UC], 69)
        acc = at("acc", [P, 2, 2, UC], 93)
        md = at("md", [P, len(TILES1), 2, GH], 28.5)
        qT = at("qT", [P, 6, S], 33)
        kT = at("kT", [P, 6, S], 45)
        V1 = at("V1", [P, TT, GROUPS, UC], 57)
        S1 = at("S1", [P, 2, 2, 2, 2 * P], 69)
        PT1 = at("PT1", [P, 2, 2, GH * P], 77)
        oT = at("oT", [P, 6, S], 85)
        stats = at("stats", [GH, 2, GROUPS, S], 0)
        cosT = at("cosT", [P, GROUPS, TT, 8], 98)
        sinT = at("sinT", [P, GROUPS, TT, 8], 98.5)
        negm = at("negm", [P, len(TILES1), GH], 99)
        alpha = at("alpha", [GH, GROUPS, S], 17)
        amax = at("amax", [GH, 2, S], 23)
        comb = at("comb", [P, 3, S], 69)
        y1 = at("y1", [P, KD, S], 33)
        hidH = at("hidH", [P, KF, S], 0, F32R)
        hidL = at("hidL", [P, KF, S], 44, F32R)
        act = at("act", [P, 4, S], 88)
        yff = at("yff", [P, KD, S], 88)
        hot = at("hot", [BUCKETS, 2 * REL], 53)
        rel = at("rel", [BUCKETS, HEADS2], 58.25)
        rrow = at("rrow", [HEADS2, REL], 58.5)
        cc = at("cc", [P, 4, S + 2], 8)
        md2 = at("md2", [P, 3, len(TILES23)], 17)
        bufAH = at("bufAH", [P, 4, S], 20, F32R)
        bufAL = at("bufAL", [P, 4, S], 28, F32R)
        bufBH = at("bufBH", [P, 4, S], 36, F32R)
        bufBL = at("bufBL", [P, 4, S], 44, F32R)
        merged = at("merged", [P, KD, S], 52)
        mgH = at("mgH", [P, KD, S], 36, F32R)
        mgL = at("mgL", [P, KD, S], 88, F32R)
        sg = at("sg", [P, 2, S], 68)
        q2 = at("q2", [P, 4, S], 72)
        k2 = at("k2", [P, 4, S], 80)
        V2 = at("V2", [P, TT, HEADS2 * DH], 88)
        W0 = at("W0", [P, 4, S], 8)
        W1 = at("W1", [P, 4, S], 96)
        S2 = at("S2", [P, 2, S], 0)
        PT2 = at("PT2", [P, 2, S], 4)
        memtok = at("memtok", [P, MEM // P, D], 72)
        memT = at("memT", [P, KD, MEM], 80)
        mk = at("mk", [P, MEM_HEADS, MEM], 88)
        mv = at("mv", [P, MEM // P, MEM_HEADS * P], 92)
        qm = at("qm", [P, 4, S], 8)
        y2 = at("y2", [P, KD, S], 72)
        otok = at("otok", [P, TT, D], 8)
        memH = bufAH[:].rearrange("p c (e m) -> p (c e) m", e=2)
        memL = bufAL[:].rearrange("p c (e m) -> p (c e) m", e=2)

        ps = ctx.enter_context(nc.psum_tensor("ps", [P, 8, 512], F32))
        scratch = nc.dram_tensor("bias_rows", (HEADS2, P, REL), F32, kind="Internal")

        ident = ident_t[:]

        def v(name, n=0, count=1):
            t, r, _ = VEC[name]
            if isinstance(n, int):
                return vec[:, t, r + n:r + n + count]
            return vec[:, t, bass.ds(n + r, count)]

        k_loaded = sem("k_loaded")
        vec_loaded = sem("vec_loaded")
        x_loaded = sem("x_loaded")
        pos_loaded = sem("pos_loaded")
        wpool_loaded = sem("wpool_loaded")
        raw_loaded = [sem("raw_loaded0"), sem("raw_loaded1")]
        ada_loaded = [sem(f"ada_loaded{i}") for i in range(3)]
        ada_summed = [sem("ada_summed_dve"), sem("ada_summed_pool")]
        ada_turned = sem("ada_turned")
        hi_done = sem("hi_done")
        lo_done = sem("lo_done")
        pe_seg = sem("pe_seg")
        banks_read = [sem("banks_read0"), sem("banks_read1")]
        ones_ready = sem("ones_ready")
        vec_turned = sem("vec_turned")
        vec_ready = sem("vec_ready")
        x_turned = sem("x_turned")
        x_ready = sem("x_ready")
        silu_exp = sem("silu_exp")
        cact_ready = sem("cact_ready")
        angle_ready = sem("angle_ready")
        trig_ready = sem("trig_ready")
        mod_ready = sem("mod_ready")
        sq_ready = sem("sq_ready")
        ss_added = sem("ss_added")
        var_ready = sem("var_ready")
        std_ready = sem("std_ready")
        diag_ready = sem("diag_ready")
        rstd_ready = sem("rstd_ready")
        scaled = sem("scaled")
        h_hi = sem("h_hi")
        h_lo = [sem("h_lo_dve"), sem("h_lo_pool")]
        shifted = sem("shifted")
        delta_ready = sem("delta_ready")
        x_added = [sem("x_added_pool"), sem("x_added_dve")]
        rope_done = sem("rope_done")
        turned = sem("turned")
        turn_read = sem("turn_read")
        s_done = sem("s_done")
        s_read = sem("s_read")
        negm_ready = sem("negm_ready")
        exp_done = sem("exp_done")
        pt_done = sem("pt_done")
        pt_read = sem("pt_read")
        pv_done = sem("pv_done")
        pv_read = sem("pv_read")
        pool_mixed = sem("pool_mixed")
        pool_done = sem("pool_done")
        pool_val = sem("pool_val")
        cat_hi = sem("cat_hi")
        cat_lo = sem("cat_lo")
        gap_ready = sem("gap_ready")
        gap_exp = sem("gap_exp")
        alpha_ready = sem("alpha_ready")
        alpha_spread = sem("alpha_spread")
        attn_ready = sem("attn_ready")
        seeded = sem("seeded")
        gate_conv = sem("gate_conv")
        val_conv = sem("val_conv")
        gelu_done = sem("gelu_done")
        hid_ready = sem("hid_ready")
        hid_hi = sem("hid_hi")
        hid_lo = sem("hid_lo")
        hot_loaded = sem("hot_loaded")
        rel_done = sem("rel_done")
        rrow_ready = sem("rrow_ready")
        rrow_stored = sem("rrow_stored")
        bias_loaded = sem("bias_loaded")
        pads_zero = sem("pads_zero")
        conv_y = sem("conv_y")
        conv_hi = sem("conv_hi")
        conv_lo = sem("conv_lo")
        s2_done = sem("s2_done")
        s2_read = sem("s2_read")
        negm2_ready = sem("negm2_ready")
        exp2_done = sem("exp2_done")
        p2_scaled = sem("p2_scaled")
        pt2_done = sem("pt2_done")
        pt2_read = sem("pt2_read")
        pv2_done = sem("pv2_done")
        o2_hi = sem("o2_hi")
        o2_lo = sem("o2_lo")
        merged_ready = sem("merged_ready")
        m_hi = sem("m_hi")
        m_lo = sem("m_lo")
        mem_loaded = sem("mem_loaded")
        mem_turned = sem("mem_turned")
        mem_ready = sem("mem_ready")
        out_turned = sem("out_turned")
        out_copied = sem("out_copied")
        out_stored = sem("out_stored")
        act_own = sem("act_own")
        dve_own = sem("dve_own")
        pool_own = sem("pool_own")

        def rows(w, k0, nk, c0):
            return w.rearrange("(k p) n -> p k n", p=P)[:, k0:k0 + nk, c0:c0 + UC]

        def unit_source(d):
            if d < D_OUT:
                if d == 0:
                    return rows(a["w_in"], 0, KD, 0), KD
                g, part = (d - 1) // 3, (d - 1) % 3
                return rows(a["w_in"], 0, KD, UC + part * 768 + g * UC), KD
            if d < D_UP1:
                return rows(a["w_out"], 0, 4, (d - D_OUT) * UC), 4
            if D_DOWN1 <= d < D_IN2 or d >= D_DOWN2:
                w, r = (a["w_down"], d - D_DOWN1) if d < D_IN2 else (a["w_down_2"], d - D_DOWN2)
                g, q = r // 4, r % 4
                return rows(w, DOWN_K0[q], DOWN_K[q], g * UC), DOWN_K[q]
            if D_UP1 <= d < D_DOWN1 or D_UP2 <= d < D_DOWN2:
                w, r = (a["w_up"], d - D_UP1) if d < D_IN2 else (a["w_up_2"], d - D_UP2)
                return rows(w, 0, KD, r % 2 * D_FF + r // 2 * UC), KD
            if d < D_BR0:
                r = d - D_IN2
                col = (512, 1024, 0, 1536, 2048, 2560)[r // 2] + r % 2 * UC
                return rows(a["w_in_2"], 0, KD, col), KD
            if D_KV <= d < D_KV + 4:
                return rows(a["w_mem_kv_2"], 0, KD, (d - D_KV) * UC), KD
            if D_KV + 4 <= d < D_BR1:
                return rows(a["w_in_2"], 0, KD, 3072 + (d - D_KV - 4) * UC), KD
            if d < D_OUT2:
                br, d0, w = next((i, x, y) for i, x, y in (
                    (2, D_BR2, a["w_mem_out_2"]), (1, D_BR1, a["w_attn_out_2"]), (0, D_BR0, a["w_conv_out_2"])) if d >= x)
                j, r = (d - d0) // 2, (d - d0) % 2
                if r == 0:
                    return rows(a["w_in_2"], 0, KD, 3584 + br * D + j * UC), KD
                return rows(w, 0, 4, j * UC), 4
            return rows(a["w_out_2"], 0, KD, (d - D_OUT2) * UC), KD

        def split_chunks(d):
            if D_UP1 <= d < D_DOWN1 + 2 or D_UP2 <= d < D_DOWN2 + 2:
                return KD
            return unit_source(d)[1]

        def tokens(t, k, g, b):
            if g == 0:
                return t[:, k, b * P:(b + 1) * P]
            return t[:, k, :].rearrange("p (i r) -> p r i", r=TT)[:, b, :]

        def key_blocks(n):
            return sum(t[2] for t in TILES1[:n])

        def pairs_before(n):
            return sum(1 for t in TILES23[:n] if t[0] == "mem" or t[2] % 2 == 1)

        steps = [("start",)] + [("squares", N_PRE1, k) for k in range(KD)] + [(f, n) for n in range(ADA_FIRST) for f in ("ada", "ada_turn")]
        steps += [("ada_end", 0), ("split", 0), ("split", 1), ("norm", N_PRE1), ("apply", N_PRE1)]
        e = 0
        for d in range(D_IN, D_OUT):
            n = ADA_FIRST + 2 * d
            for m in range(2):
                steps += [("seg", d, m)]
                if 0 < 2 * d + m <= ADA_REST:
                    steps += [("ada_turn", n + m - 1)]
                if 2 * d + m < ADA_REST:
                    steps += [("ada", n + m)]
            steps += [("split", d + 2), ("evac_in", d)]
            if d == ADA_REST // 2 - 1:
                steps += [("windows",)]
            if d >= 2 and (d - 1) % 3 in (1, 2):
                steps += [("turn", e)]
                e += 1
        steps += [("ada_end", 1), ("front", 0), ("pool",), ("front", 1)]
        for n in range(len(TILES1)):
            steps += [("mid", n)]
            if n + 2 < len(TILES1):
                steps += [("front", n + 2)]
            steps += [("back", n)]
        steps += [("combine",)]
        def with_squares(d0, d1, per, n):
            out, late = [], []
            for d in range(d0, d1):
                out += [("seg", d, 0), ("seg", d, 1)] + late
                late = []
                if d + 2 < D_END:
                    out += [("split", d + 2)]
                if (d - d0) % per == per - 1:
                    c = 2 * ((d - d0) // per)
                    out += [("evac_y", d)]
                    late = [("squares", n, c), ("squares", n, c + 1)]
            return out + late

        def residual(n, nxt, between=()):
            return [("norm", n), ("resid", n), *between] + [("squares", nxt, k) for k in range(KD)] + [("norm", nxt), ("apply", nxt)]

        steps += with_squares(D_OUT, D_UP1, 1, N_POST1) + residual(N_POST1, N_PREF1) + [("up", 0)]
        steps += with_squares(D_DOWN1, D_IN2, 4, N_POSTF1) + residual(N_POSTF1, N_PRE2) + [("bias_fetch",)]
        for d in range(D_IN2, D_BR0):
            steps += [("seg", d, 0), ("seg", d, 1), ("split", d + 2), ("evac_in2", d)]
            if d == D_IN2 + 1:
                steps += [("bias_rows",)]
        steps += [("bias_load",)]

        def branch(d0):
            out = []
            for d in range(d0, d0 + 8):
                out += [("seg", d, 0), ("seg", d, 1), ("split", d + 2), ("evac_br", d)]
            return out

        def branch_pieces(d0):
            out, late = [], []
            for d in range(d0, d0 + 8):
                nk = unit_source(d)[1]
                for m in range(2):
                    for k in range(0, nk, 2):
                        out += [[("seg", d, m, k, k + 2)] + late]
                        late = []
                out[-1] += [("split", d + 2)]
                late = [("evac_br", d)]
            out[-1] += late
            return out

        def attend(first, last, pieces):
            tiles = [("front2", first), ("front2", first + 1)]
            for n in range(first, last):
                tiles += [("mid2", n)]
                if n > first:
                    tiles += [("lo2", n - 1)]
                if n + 2 < last:
                    tiles += [("front2", n + 2)]
                tiles += [("back2", n)]
            tiles += [("lo2", last - 1)]
            out = []
            for i, tile in enumerate(tiles):
                out += [tile]
                for piece in pieces[i * len(pieces) // len(tiles):(i + 1) * len(pieces) // len(tiles)]:
                    out += piece
            return out

        pieces = branch_pieces(D_BR0)
        beside, turned_beside = pieces[-10:-6], pieces[-6:]
        steps += attend(0, len(TILES2), pieces[:-10])
        steps += [("mem_load",)] + sum(beside, []) + [("mem_turn",)] + sum(turned_beside, [])
        steps += [("squares", N_MEM, k) for k in range(KD)] + [("norm", N_MEM), ("apply", N_MEM)]
        for d in range(D_KV, D_BR1):
            steps += [("seg", d, 0), ("seg", d, 1), ("split", d + 2), ("evac_kv", d)]
        steps += attend(len(TILES2), len(TILES23), branch_pieces(D_BR1))
        for step in branch(D_BR2):
            steps += [step]
            if step[0] == "evac_br" and step[1] % 2 == 1:
                steps += [("merge", step[1] - D_BR2 - 1), ("merge", step[1] - D_BR2)]
        steps += with_squares(D_OUT2, D_UP2, 1, N_POST2) + residual(N_POST2, N_PREF2) + [("up", 1)]
        steps += with_squares(D_DOWN2, D_END, 4, N_POSTF2) + [("norm", N_POSTF2), ("resid", N_POSTF2), ("finish",)]

        def wait_x(eng, n, k):
            r = RESID[n]
            if k % 3 == 2:
                eng.wait_ge(x_added[1], 2 * r + k // 3 + 1)
            else:
                eng.wait_ge(x_added[0], 6 * r + k + 1 - (k + 1) // 3)

        def wait_h(eng, n, k):
            eng.wait_ge(h_lo[k % 2], KD // 2 * SPLITS[n] + k // 2 + 1)

        def walk(handlers):
            for step in steps:
                f = handlers.get(step[0])
                if f is not None:
                    f(*step[1:])

        def y_of(d):
            if d < D_UP1:
                return y1, 2 * (d - D_OUT)
            if d < D_IN2:
                return yff, 2 * ((d - D_DOWN1) // 4)
            if d < D_UP2:
                return y2, 2 * (d - D_OUT2)
            return yff, 2 * ((d - D_DOWN2) // 4)

        def banks(d):
            p = pair_of(d)
            return ps[:, 2 * p:2 * p + 2, :]

        norm_source = {
            N_PRE1: (xT, S), N_POST1: (y1, S), N_PREF1: (xT, S), N_POSTF1: (yff, S), N_PRE2: (xT, S),
            N_MEM: (memT, MEM), N_POST2: (y2, S), N_PREF2: (xT, S), N_POSTF2: (yff, S)}
        gains = {
            N_PRE1: colA[:, 0, :], N_POST1: colA[:, 1, :], N_PREF1: colA[:, 2, :], N_POSTF1: colA[:, 3, :],
            N_PRE2: v("g_pre_mix_2", 0, 8), N_MEM: v("g_mem_2", 0, 8), N_POST2: v("g_post_mix_2", 0, 8),
            N_PREF2: v("g_pre_ffn_2", 0, 8), N_POSTF2: v("g_post_ffn_2", 0, 8)}
        shifts = {N_PRE1: mod[:, 0:8], N_PREF1: mod[:, 24:32]}
        y_units = {N_POST1: D_OUT, N_POST2: D_OUT2, N_POSTF1: D_DOWN1, N_POSTF2: D_DOWN2}

        def tile2(n):
            kind, i, h, nb = TILES23[n]
            return (kind, i, h, nb, h // 2, DH * (h % 2)) if kind == "self" else (kind, i, h, nb, h, 0)

        block = ctx.enter_context(nc.Block())

        @block.sync
        def _(sp):
            def load(d):
                src, nk = unit_source(d)
                if d >= 2:
                    sp.wait_ge(lo_done, d - 1)
                sp.dma_start(raw[:, d % 2, 0:nk, :], src).then_inc(raw_loaded[d % 2], 16)

            def ada(n):
                if n >= 3:
                    for used in ada_summed:
                        sp.wait_ge(used, n - 2)
                sp.dma_start(adaw[:, n % 3, :, :], rows(a["w_ada"], 0, KD, n * UC)).then_inc(ada_loaded[n % 3], 16)

            def up(w, d0):
                cols = w.rearrange("(k p) n -> p k n", p=P)
                with sp.Fori(0, FF_PAIRS) as j:
                    for half in range(2):
                        sp.wait_ge(lo_done, j * 2 + (d0 + half - 1))
                        sp.dma_start(raw[:, half, :, :], cols[:, :, bass.ds(j * UC + half * D_FF, UC)]
                                     ).then_inc(raw_loaded[half], 16)

            def dense(d0, d1):
                for d in range(d0, d1):
                    load(d)

            for n in range(ADA_FIRST):
                ada(n)
            dense(0, 2)
            for d in range(2, D_OUT):
                ada(ADA_FIRST + 2 * (d - 2))
                ada(ADA_FIRST + 2 * (d - 2) + 1)
                load(d)
            dense(D_OUT, D_UP1)
            up(a["w_up"], D_UP1)
            dense(D_DOWN1, D_UP2)
            up(a["w_up_2"], D_UP2)
            dense(D_DOWN2, D_END)
            for t in range(TT):
                sp.wait_ge(out_copied, t + 1)
                sp.dma_start(out[t * P:(t + 1) * P, :], otok[:, t, :]).then_inc(out_stored, 16)
            sp.wait_ge(out_stored, 16 * TT)

        @block.gpsimd
        def _(pool):
            def cut(d):
                nk = split_chunks(d)
                pool.wait_ge(hi_done, d + 1)
                pool.tensor_tensor(WL[:, d % 2, 0:nk, :], raw[:, d % 2, 0:nk, :],
                                   WH[:, d % 2, 0:nk, :].bitcast(F32), ALU.subtract).then_inc(lo_done, 1)

            own = [0]

            def link(ins):
                own[0] += 1
                ins.then_inc(pool_own, 1)
                pool.wait_ge(pool_own, own[0])

            def ada(n):
                if n == 0:
                    pool.wait_ge(cact_ready, 1)
                pool.wait_ge(ada_loaded[n % 3], 16 * (n // 3 + 1))
                if n >= 2:
                    pool.wait_ge(ada_turned, n - 1)
                k = KD - 1
                out = acc[:, n % 2, 1, :]
                ins = pool.tensor_scalar(out, adaw[:, n % 3, k, :], small[:, 32 + k:33 + k], None, ALU.mult)
                if n < ADA_FIRST:
                    k, w = KD - 2, adaw[:, n % 3, KD - 2, :]
                    link(ins)
                    link(pool.tensor_scalar(w, w, small[:, 32 + k:33 + k], None, ALU.mult))
                    ins = pool.tensor_tensor(out, out, w, ALU.add)
                ins.then_inc(ada_summed[1], 1)

            def resid(n):
                for k in range(KD):
                    if k % 3 == 2:
                        continue
                    pool.wait_ge(delta_ready, KD * RESID[n] + k + 1)
                    pool.tensor_tensor(xT[:, k, :], xT[:, k, :], dl[:, k % 4, :], ALU.add).then_inc(x_added[0], 1)

            def apply(n):
                w = norm_source[n][1]
                hi, lo = (memH, memL) if n == N_MEM else (hH, hL)
                for k in range(1, KD, 2):
                    pool.wait_ge(h_hi, KD * SPLITS[n] + k + 1)
                    pool.tensor_tensor(lo[:, k, :], dl[:, k % 4, 0:w], hi[:, k, :].bitcast(F32), ALU.subtract
                                       ).then_inc(h_lo[1], 1)

            def up(f):
                d0 = (D_UP1, D_UP2)[f]
                with pool.Fori(0, FF_PAIRS) as j:
                    for half in range(2):
                        pool.wait_ge(hi_done, j * 2 + (d0 + 2 + half + 1))
                        pool.tensor_tensor(WL[:, half, :, :], raw[:, half, :, :],
                                           WH[:, half, :, :].bitcast(F32), ALU.subtract).then_inc(lo_done, 1)

            def windows():
                pool.wait_ge(banks_read[0], 1)
                pool.wait_ge(k_loaded, 32)
                for k in (KD - 2, KD - 1):
                    wait_h(pool, N_PRE1, k)
                end = POOL_PAD + S
                for m in range(2):
                    A, B = win[:, 0, :], win[:, 1, :]
                    link(pool.tensor_tensor(A[:, 1:end], u[:, m, 1:end], u[:, m, 0:end - 1], ALU.add))
                    link(pool.tensor_tensor(B[:, 3:end], A[:, 3:end], A[:, 1:end - 2], ALU.add))
                    if m == 1:
                        link(pool.tensor_tensor(A[:, 7:end], B[:, 7:end], B[:, 3:end - 4], ALU.add))
                        link(pool.tensor_tensor(B[:, 15:end], A[:, 15:end], A[:, 7:end - 8], ALU.add))
                    for half, t in ((0, A), (1, B)):
                        r = slice(64 * half, 64 * half + 64)
                        rc = K[r, C_RC + 16 * m:C_RC + 16 * m + 16]
                        link(pool.tensor_tensor(t[r, 16:32], t[r, 16:32], rc, ALU.mult))
                        pool.tensor_tensor(u[r, m, 16:32], t[r, 16:32], u[r, m, 16:32], ALU.subtract).then_inc(pool_mixed, 1)
                        link(pool.tensor_scalar(t[r, 32:end], t[r, 32:end], K[r, C_RW + m:C_RW + m + 1], None, ALU.mult))
                        pool.tensor_tensor(u[r, m, 32:end], t[r, 32:end], u[r, m, 32:end], ALU.subtract).then_inc(pool_mixed, 1)
                    pool.wait_ge(pool_mixed, 4 * m + 4)
            walk({"split": cut, "windows": windows, "ada": ada, "resid": resid, "apply": apply, "up": up})

        @block.scalar
        def _(sc):
            own = [0]

            def link(ins):
                own[0] += 1
                ins.then_inc(act_own, 1)
                sc.wait_ge(act_own, own[0])

            def start():
                sc.dma_start(ident_t[:], a["table"][:, C_ID:C_ID + P]).then_inc(k_loaded, 16)
                for name, (t, r, n) in VEC.items():
                    src = {"ffn_conv_w_2b": "ffn_conv_w_2"}.get(name, name)
                    flat = a[src]
                    off = 88 if name == "ffn_conv_w_2b" else 0
                    sc.dma_start(vrow[r:r + n, t, :], flat[off:off + n, :]).then_inc(vec_loaded, 16)
                for t in range(TT):
                    sc.dma_start(xtok[:, t, :], a["x"][t * P:(t + 1) * P, :]).then_inc(x_loaded, 16)
                sc.dma_start(K[:], a["table"][:, P:C_END]).then_inc(k_loaded, 16)
                sc.dma_start(posi[:], a["positions"]).then_inc(pos_loaded, 16)
                sc.dma_start(wpool[:], a["w_pool"].rearrange("(m g) c d -> (g c) m d", g=2)).then_inc(wpool_loaded, 16)
                sc.wait_ge(vec_ready, 4)
                sc.activation(small[:, 0:8], v("c", 0, 8), ACT.Exp, scale=-1.0).then_inc(silu_exp, 1)
                sc.wait_ge(angle_ready, 2)
                sc.activation(sinT[:].rearrange("p g t f -> p (g t) f"), trig[:, 2, :, :], ACT.Sin).then_inc(trig_ready, 1)
                sc.activation(cosT[:].rearrange("p g t f -> p (g t) f"), trig[:, 3, :, :], ACT.Sin).then_inc(trig_ready, 1)

            def split(d):
                r = d
                nk = split_chunks(d)
                sc.wait_ge(raw_loaded[r % 2], 16 * (r // 2 + 1))
                if d >= 2:
                    sc.wait_ge(pe_seg, 2 * (d - 2) + 2)
                sc.activation(WH[:, d % 2, 0:nk, :], raw[:, d % 2, 0:nk, :], ACT.Copy).then_inc(hi_done, 1)

            def squares(n, k):
                src, w = norm_source[n]
                m = KD * n + k
                if n == N_PRE1:
                    sc.wait_ge(x_ready, k + 1)
                elif n == N_MEM:
                    sc.wait_ge(mem_ready, k + 1)
                elif n in y_units:
                    d = y_units[n] + (k // 2 if n in (N_POST1, N_POST2) else 4 * (k // 2))
                    sc.wait_ge(banks_read[pair_of(d)], bank_use(d) + 1)
                else:
                    wait_x(sc, n - 1 if n != N_PRE2 else N_POSTF1, k)
                if m >= 2:
                    sc.wait_ge(ss_added, m - 1)
                sc.activation(sq[:, k % 2, 0:w], src[:, k, :], ACT.Square).then_inc(sq_ready, 1)
                if k == KD - 1:
                    sc.wait_ge(ones_ready, 1)
                    link(sc.activation(small[:, 56:57], ones[:, 0:1], ACT.Sqrt))

            def norm(n):
                c = norm_source[n][1] // P
                sc.wait_ge(var_ready, n + 1)
                sc.activation(nt[:, 0, 4:4 + c], nt[:, 0, 0:c], ACT.Sqrt).then_inc(std_ready, 1)

            def apply(n):
                w = norm_source[n][1]
                dst = memH if n == N_MEM else hH
                for k in range(KD):
                    t = dl[:, k % 4, 0:w]
                    sc.wait_ge(scaled, KD * SPLITS[n] + k + 1)
                    if n in shifts:
                        sc.activation(t, t, ACT.Identity, bias=shifts[n][:, k:k + 1]).then_inc(shifted, 1)
                        sc.wait_ge(shifted, KD * (1 if n == N_PREF1 else 0) + k + 1)
                    sc.activation(dst[:, k, :], t, ACT.Copy).then_inc(h_hi, 1)

            def evac_in(d):
                sc.wait_ge(pe_seg, 2 * d + 2)
                if d == 0:
                    sc.wait_ge(pads_zero, 1)
                    ins = sc.activation(u[:, :, POOL_PAD:], banks(d), ACT.Copy)
                else:
                    g, part = (d - 1) // 3, (d - 1) % 3
                    src = banks(d).rearrange("p b (t n) -> p (b t) n", t=2)
                    if part == 2:
                        ins = sc.activation(V1[:, :, g, :], src, ACT.Copy)
                    else:
                        e = 2 * g + part
                        if e >= 2:
                            sc.wait_ge(turned, 2 * (e - 1))
                        ins = sc.activation(qtok[:, e % 2, :, :], src, ACT.Copy)
                ins.then_inc(banks_read[pair_of(d)], 1)

            def turn(e):
                dst = qT if e % 2 == 0 else kT
                for hp in range(2):
                    sc.wait_ge(turned, 2 * e + hp + 1)
                    sc.activation(dst[:, 2 * (e // 2) + hp, :], ps[:, 5 + hp, :], ACT.Copy).then_inc(turn_read, 1)

            def pool_step():
                for m in range(2):
                    sc.wait_ge(pool_done, m + 1)
                    for half in range(2):
                        r = slice(64 * half, 64 * half + 64)
                        ins = sc.activation(win[r, m, 0:S], ps[r, 2 * m + half, :], ACT.Identity,
                                            bias=small[r, 16 + m:17 + m], scale=v("pool_scale", m)[r, :])
                        ins.then_inc(pool_val, 1)
                    sc.wait_ge(pool_val, 2 * m + 2)
                    sc.activation(hH[:, m, :], win[:, m, 0:S], ACT.Copy).then_inc(cat_hi, 1)

            def front(n):
                sc.wait_ge(negm_ready, n + 1)
                w = P * TILES1[n][2]
                for x in range(GH):
                    t = S1[:, n % 2, x // 2, x % 2, 0:w]
                    sc.activation(t, t, ACT.Exp, bias=negm[:, n, x:x + 1], scale=DH ** -0.5,
                                  accum_out=md[:, n, 1, x:x + 1]).then_inc(exp_done, 1)

            def mid(n):
                if n >= 2:
                    sc.wait_ge(pv_done, n - 1)
                for kb in range(TILES1[n][2]):
                    sc.wait_ge(pt_done, key_blocks(n) + kb + 1)
                    sc.activation(PT1[:, n % 2, kb, :], ps[:, 6, :], ACT.Copy).then_inc(pt_read, 1)

            def combine():
                sc.wait_ge(gap_ready, 1)
                sc.activation(alpha[:], alpha[:], ACT.Exp, scale=DH ** -0.5).then_inc(gap_exp, 1)
                for hp in range(2):
                    sc.wait_ge(attn_ready, hp + 1)
                    sc.activation(hH[:, 2 + hp, :], comb[:, 0, :], ACT.Copy).then_inc(cat_hi, 1)

            def evac_y(d):
                sc.wait_ge(pe_seg, 2 * d + 2)
                y, c = y_of(d)
                sc.activation(y[:, c:c + 2, :], banks(d), ACT.Copy).then_inc(banks_read[pair_of(d)], 1)

            def up(f):
                d0 = (D_UP1, D_UP2)[f]
                t0 = 4 * FF_PAIRS if f else 0
                with sc.Fori(0, FF_PAIRS) as j:
                    def cut(half):
                        d = d0 + 2 + half
                        sc.wait_ge(raw_loaded[half], j * 16 + 16 * (d // 2 + 1))
                        sc.wait_ge(pe_seg, j * 4 + 2 * (d - 2) + 2)
                        sc.activation(WH[:, half, :, :], raw[:, half, :, :], ACT.Copy).then_inc(hi_done, 1)

                    def seed(m, half):
                        if f == 0:
                            w2, b = v("conv_w", j * 2 + (44 + m)), v("conv_b", j * 2 + m)
                        else:
                            c = j * 2 + (22 * half + m)
                            w2, b = v("ffn_conv_w_2b", c), v("ffn_conv_b_2", c)
                        sc.activation(act[:, 2 * half + m, :], ps[:, 2 * half + m, :], ACT.Identity,
                                      bias=b, scale=w2).then_inc(seeded, 1)

                    sc.wait_ge(hid_lo, j * 2 + (2 + 2 * FF_PAIRS * f))
                    sc.wait_ge(pe_seg, j * 4 + 2 * d0 + 1)
                    seed(0, 0)
                    sc.wait_ge(pe_seg, j * 4 + 2 * d0 + 2)
                    seed(1, 0)
                    cut(0)
                    for m in range(2):
                        sc.wait_ge(gate_conv, j * 2 + (m + 3 + 2 * FF_PAIRS * f))
                        sc.activation(act[:, m, :], act[:, m, :], ACT.Gelu_apprx_tanh).then_inc(gelu_done, 1)
                    if f == 1:
                        for m in range(2):
                            sc.wait_ge(pe_seg, j * 4 + 2 * d0 + 3 + m)
                            seed(m, 1)
                    cut(1)
                    for m in range(2):
                        sc.wait_ge(hid_ready, j * 2 + (m + 3 + 2 * FF_PAIRS * f))
                        sc.activation(hidH[:, bass.ds(j * 2 + m, 1), :], act[:, m:m + 1, :], ACT.Copy).then_inc(hid_hi, 1)

            def bias_fetch():
                wait_x(sc, N_POSTF1, KD - 1)
                sc.dma_start(hot[:], a["hot"]).then_inc(hot_loaded, 16)
                sc.dma_start(rel[:], a["rel_bias_2"]).then_inc(hot_loaded, 16)

            def bias_rows():
                sc.wait_ge(rrow_ready, 2)
                sc.dma_start(scratch.ap(), rrow[:].unsqueeze(1).broadcast_to([HEADS2, P, REL])).then_inc(rrow_stored, 16)

            def evac_in2(d):
                r = d - D_IN2
                kind, j = r // 2, r % 2
                if kind == 0:
                    sc.wait_ge(pe_seg, 2 * d + 2)
                    sc.activation(cc[:, 2 * j:2 * j + 2, 2:], banks(d), ACT.Copy).then_inc(banks_read[d % 2], 1)
                elif kind == 2:
                    for m in range(2):
                        c = 2 * j + m
                        sc.wait_ge(*((banks_read[j], bank_use(d) + 1) if m else (conv_y, j + 1)))
                        sc.activation(bufAH[:, c, :], sq[:, m, :], ACT.Copy).then_inc(conv_hi, 1)
                elif kind >= 3:
                    sc.wait_ge(pe_seg, 2 * d + 2)
                    if kind == 5:
                        ins = sc.activation(V2[:, :, UC * j:UC * j + UC],
                                            banks(d).rearrange("p b (t n) -> p (b t) n", t=2), ACT.Copy)
                    else:
                        ins = sc.activation((q2, k2)[kind - 3][:, 2 * j:2 * j + 2, :], banks(d), ACT.Copy)
                    ins.then_inc(banks_read[d % 2], 1)

            def bias_load():
                sc.wait_ge(rrow_stored, 16)
                sc.wait_ge(conv_lo, 4)
                for i, w in enumerate((W0, W1)):
                    src = bass.AP(tensor=scratch, offset=4 * i * P * REL + P - 1, ap=[[REL - 1, P], [P * REL, 4], [1, S]])
                    sc.dma_start(w[:], src).then_inc(bias_loaded, 16)

            def evac_br(d):
                br = next(i for i, d0 in ((2, D_BR2), (1, D_BR1), (0, D_BR0)) if d >= d0)
                j, r = (d - (D_BR0, D_BR1, D_BR2)[br]) // 2, (d - D_BR0) % 2
                if r:
                    return
                for m in range(2):
                    c = 2 * j + m
                    sc.wait_ge(pe_seg, 2 * d + 1 + m)
                    n = 8 * br + c
                    if n >= 2:
                        sc.wait_ge(merged_ready, n - 1)
                    ins = sc.activation(sg[:, m, :], ps[:, 2 * pair_of(d) + m, :], ACT.Sigmoid,
                                        bias=v("b_gate_2", 8 * br + c))
                    if m == 0:
                        link(ins)
                ins.then_inc(banks_read[pair_of(d)], 1)

            def front2(n):
                kind, i, h, nb, _, _ = tile2(n)
                sc.wait_ge(negm2_ready, n + 1)
                if kind == "self":
                    t, scale = S2[:, n % 2, 0:P * nb], 1.0
                    src = t
                else:
                    t, scale = S2[:, n % 2, 0:P * nb], P ** -0.5
                    src = ps[:, 4 + n % 2, 0:P * nb]
                sc.activation(t, src, ACT.Exp, bias=md2[:, 0, n:n + 1], scale=scale,
                              accum_out=md2[:, 1, n:n + 1]).then_inc(exp2_done, 1)

            def mid2(n):
                nb = tile2(n)[3]
                sc.wait_ge(pt2_done, n + 1)
                if n >= 2:
                    sc.wait_ge(pv2_done, n - 1)
                sc.activation(PT2[:, n % 2, 0:P * nb], ps[:, 6, 0:P * nb], ACT.Copy).then_inc(pt2_read, 1)

            def back2(n):
                kind, i, h, _, c, row = tile2(n)
                if kind == "self" and row == 0:
                    return
                sc.wait_ge(pv2_done, n + 1)
                dst = bufBH if kind == "self" else bufAH
                sc.activation(dst[:, c, i * P:(i + 1) * P], ps[:, 7, 0:P], ACT.Copy).then_inc(o2_hi, 1)

            def mem_load():
                sc.wait_ge(pv2_done, len(TILES2))
                for t in range(MEM // P):
                    sc.dma_start(memtok[:, t, :], a["mem_2"][t * P:(t + 1) * P, :]).then_inc(mem_loaded, 16)

            def mem_turn():
                for k in range(KD):
                    sc.wait_ge(mem_turned, k + 1)
                    sc.activation(memT[:, k, :], ps[:, 6 + k % 2, 0:MEM], ACT.Copy).then_inc(mem_ready, 1)

            def evac_kv(d):
                r = d - D_KV
                sc.wait_ge(pe_seg, 2 * d + 2)
                if r < 2:
                    ins = sc.activation(mk[:, 2 * r:2 * r + 2, :], banks(d)[:, :, 0:MEM], ACT.Copy)
                elif r < 4:
                    ins = sc.activation(mv[:, :, UC * (r - 2):UC * (r - 1)], banks(d)[:, :, 0:UC], ACT.Copy)
                else:
                    ins = sc.activation(qm[:, 2 * (r - 4):2 * (r - 3), :], banks(d), ACT.Copy)
                ins.then_inc(banks_read[d % 2], 1)

            def merge(c):
                sc.wait_ge(merged_ready, 16 + c + 1)
                sc.activation(mgH[:, c, :], merged[:, c, :], ACT.Copy).then_inc(m_hi, 1)

            walk({"start": start, "split": split, "squares": squares, "norm": norm, "apply": apply,
                  "evac_in": evac_in, "turn": turn,
                  "pool": pool_step, "front": front, "mid": mid, "combine": combine, "evac_y": evac_y, "up": up,
                  "bias_fetch": bias_fetch, "bias_rows": bias_rows, "evac_in2": evac_in2, "bias_load": bias_load, "evac_br": evac_br,
                  "front2": front2, "mid2": mid2, "back2": back2, "mem_load": mem_load, "mem_turn": mem_turn,
                  "evac_kv": evac_kv, "merge": merge})

        @block.vector
        def _(ve):
            own = [0]

            def link(ins):
                own[0] += 1
                ins.then_inc(dve_own, 1)
                ve.wait_ge(dve_own, own[0])

            def start():
                ve.memset(ones[:], 1.0).then_inc(ones_ready, 1)
                for t, r in enumerate(TABLE_ROWS):
                    if t == 0:
                        ve.wait_ge(vec_turned, 1)
                    ve.tensor_copy(vec[:, t, 0:r], ps[:, 4, t * P:t * P + r]).then_inc(vec_ready, 1)
                ve.wait_ge(vec_ready, 4)
                ve.wait_ge(k_loaded, 32)
                ve.wait_ge(silu_exp, 1)
                link(ve.tensor_scalar(small[:, 8:16], small[:, 0:8], 1.0, None, ALU.add))
                link(ve.reciprocal(small[:, 24:32], small[:, 8:16]))
                ve.tensor_tensor(small[:, 32:40], small[:, 24:32], v("c", 0, 8), ALU.mult).then_inc(cact_ready, 1)
                link(ve.tensor_tensor(small[:, 16:18], v("b_pool", 0, 2), v("pool_scale", 0, 2), ALU.mult))
                ve.wait_ge(pos_loaded, 16)
                link(ve.tensor_copy(posf[:], posi[:]))
                nb = GROUPS * TT
                link(ve.tensor_tensor(trig[:, 0, :, :], posf[:].unsqueeze(2).broadcast_to([P, nb, 8]),
                                      K[:, C_FREQ:C_FREQ + 8].unsqueeze(1).broadcast_to([P, nb, 8]), ALU.mult))
                c1 = 6.28125
                c2 = float(int((TWO_PI - c1) * 2 ** 20)) / 2 ** 20
                c3 = TWO_PI - c1 - c2
                for out_row, turns in ((2, 0.0), (3, 0.25)):
                    link(ve.tensor_scalar(trig[:, 1, :, :], trig[:, 0, :, :], 1.0 / TWO_PI, turns, ALU.mult, ALU.add))
                    link(ve.tensor_scalar(trig[:, 1, :, :], trig[:, 1, :, :], MAGIC, None, ALU.add))
                    link(ve.tensor_scalar(trig[:, 1, :, :], trig[:, 1, :, :], -MAGIC, None, ALU.add))
                    prev = trig[:, 0, :, :]
                    for c in (c1, c2, c3):
                        link(ve.scalar_tensor_tensor(out=trig[:, 4, :, :], in0=trig[:, 1, :, :], scalar=-c,
                                                     in1=prev, op0=ALU.mult, op1=ALU.add))
                        prev = trig[:, 4, :, :]
                    link(ve.tensor_scalar(trig[:, 4, :, :], trig[:, 4, :, :], turns * TWO_PI, 3.1415925, ALU.add, ALU.min))
                    ve.tensor_scalar(trig[:, out_row, :, :], trig[:, 4, :, :], -3.1415925, None, ALU.max
                                     ).then_inc(angle_ready, 1)
                for k in range(KD):
                    ve.wait_ge(x_turned, k + 1)
                    ve.tensor_copy(xT[:, k, :], ps[:, k % 3, :]).then_inc(x_ready, 1)
                ve.wait_ge(x_ready, KD)
                for i, count in enumerate((gate_conv, val_conv, hid_ready, hid_lo)):
                    for m in range(2):
                        ve.memset(small[:, 40 + 4 * m + i:41 + 4 * m + i], 0.0).then_inc(count, 1)

            def ada(n):
                if n == 0:
                    ve.wait_ge(cact_ready, 1)
                ve.wait_ge(ada_loaded[n % 3], 16 * (n // 3 + 1))
                if n >= 2:
                    ve.wait_ge(ada_turned, n - 1)
                last = KD - (3 if n < ADA_FIRST else 2)
                for k in range(last + 1):
                    w, c = adaw[:, n % 3, k, :], small[:, 32 + k:33 + k]
                    if k == 0:
                        ins = ve.tensor_scalar(acc[:, n % 2, 0, :], w, c, None, ALU.mult)
                    else:
                        ins = ve.scalar_tensor_tensor(out=acc[:, n % 2, 0, :], in0=w, scalar=c,
                                                      in1=acc[:, n % 2, 0, :], op0=ALU.mult, op1=ALU.add)
                    if k < last:
                        link(ins)
                ins.then_inc(ada_summed[0], 1)

            def ada_end(part):
                ve.wait_ge(ada_turned, ADA_FIRST if part == 0 else ADA_FIRST + ADA_REST)
                c0, c1 = (0, 16) if part == 0 else (16, 48)
                link(ve.tensor_tensor(mod[:, c0:c1], ps[:, 3 if part == 0 else 7, c0:c1], v("b_ada", c0, c1 - c0), ALU.add))
                if part == 0:
                    ve.scalar_tensor_tensor(out=colA[:, 0, :], in0=mod[:, 8:16], scalar=1.0, in1=v("g_pre_mix", 0, 8),
                                            op0=ALU.add, op1=ALU.mult).then_inc(mod_ready, 1)
                    ve.wait_ge(mod_ready, 1)
                else:
                    ve.tensor_tensor(colA[:, 1, :], mod[:, 16:24], v("g_post_mix", 0, 8), ALU.mult).then_inc(mod_ready, 1)
                    ve.scalar_tensor_tensor(out=colA[:, 2, :], in0=mod[:, 32:40], scalar=1.0, in1=v("g_pre_ffn", 0, 8),
                                            op0=ALU.add, op1=ALU.mult).then_inc(mod_ready, 1)
                    ve.tensor_tensor(colA[:, 3, :], mod[:, 40:48], v("g_post_ffn", 0, 8), ALU.mult).then_inc(mod_ready, 1)
                    ve.wait_ge(mod_ready, 4)

            def norm(n):
                c = norm_source[n][1] // P
                ve.wait_ge(ss_added, KD * n + KD)
                own_sums = nt[:, 1, 0:c * P].rearrange("p (t q) -> p t q", t=c)
                link(ve.tensor_tensor(own_sums, ps[:, 5, 0:c * P].rearrange("p (t q) -> p t q", t=c),
                                      ident.unsqueeze(1).broadcast_to([P, c, P]), ALU.mult))
                link(ve.tensor_reduce(nt[:, 0, 12:12 + c], own_sums, X, ALU.add))
                ve.tensor_scalar(nt[:, 0, 0:c], nt[:, 0, 12:12 + c], 1.0 / D, EPS, ALU.mult, ALU.add).then_inc(var_ready, 1)
                ve.wait_ge(std_ready, n + 1)
                link(ve.reciprocal(nt[:, 0, 8:8 + c], nt[:, 0, 4:4 + c]))
                for t in range(c):
                    ins = ve.tensor_scalar(nt[:, 1, t * P:(t + 1) * P], ident, nt[:, 0, 8 + t:9 + t], None, ALU.mult)
                ins.then_inc(diag_ready, 1)
                ve.wait_ge(rstd_ready, n + 1)

            def apply(n):
                src, w = norm_source[n]
                hi, lo = (memH, memL) if n == N_MEM else (hH, hL)
                for k in range(KD + 2):
                    if k < KD:
                        if k >= 4:
                            wait_h(ve, n, k - 4)
                        ve.scalar_tensor_tensor(out=dl[:, k % 4, 0:w], in0=src[:, k, :], scalar=gains[n][:, k:k + 1],
                                                in1=ps[:, 4, 0:w], op0=ALU.mult, op1=ALU.mult).then_inc(scaled, 1)
                    i = k - 2
                    if i >= 0 and i % 2 == 0:
                        ve.wait_ge(h_hi, KD * SPLITS[n] + i + 1)
                        ve.tensor_tensor(lo[:, i, :], dl[:, i % 4, 0:w], hi[:, i, :].bitcast(F32), ALU.subtract
                                         ).then_inc(h_lo[0], 1)

            def resid(n):
                src, w = norm_source[n]
                for k in range(KD):
                    if k >= 4:
                        wait_x(ve, n, k - 4)
                    ve.scalar_tensor_tensor(out=dl[:, k % 4, :], in0=src[:, k, :], scalar=gains[n][:, k:k + 1],
                                            in1=ps[:, 4, :], op0=ALU.mult, op1=ALU.mult).then_inc(delta_ready, 1)
                    if k % 3 == 2:
                        ve.wait_ge(delta_ready, KD * RESID[n] + k + 1)
                        ve.tensor_tensor(xT[:, k, :], xT[:, k, :], dl[:, k % 4, :], ALU.add).then_inc(x_added[1], 1)

            def evac_in(d):
                if d == 0:
                    for k in (KD - 2, KD - 1):
                        wait_h(ve, N_PRE1, k)
                    ve.memset(u[:, :, 0:POOL_PAD], 0.0).then_inc(pads_zero, 1)

            def turn(e):
                g, part = e // 2, e % 2
                d = 1 + 3 * g + part
                ve.wait_ge(banks_read[pair_of(d)], bank_use(d) + 1)
                ve.wait_ge(trig_ready, 2)
                q = qtok[:, e % 2, :, :].rearrange("p t (h f) -> p t h f", h=GH)
                t1, t2 = q[:, :, :, 0:8], q[:, :, :, 8:16]
                cos = cosT[:, g, :, :].unsqueeze(2).broadcast_to([P, TT, GH, 8])
                sin = sinT[:, g, :, :].unsqueeze(2).broadcast_to([P, TT, GH, 8])
                if e:
                    ve.wait_ge(rope_done, 2 * e)
                for i, (x, y) in enumerate(((t1, cos), (t2, sin), (t2, cos), (t1, sin))):
                    ins = ve.tensor_tensor(rope[:, i, :, :, :], x, y, ALU.mult)
                link(ins)
                ve.tensor_tensor(t1, rope[:, 0, :, :, :], rope[:, 1, :, :, :], ALU.subtract).then_inc(rope_done, 1)
                ve.tensor_tensor(t2, rope[:, 2, :, :, :], rope[:, 3, :, :, :], ALU.add).then_inc(rope_done, 1)

            def pool_step():
                for m in range(2):
                    ve.wait_ge(cat_hi, m + 1)
                    ve.tensor_tensor(hL[:, m, :], win[:, m, 0:S], hH[:, m, :].bitcast(F32), ALU.subtract).then_inc(cat_lo, 1)

            def front(n):
                g, b, nk = TILES1[n]
                w = P * nk
                ve.wait_ge(s_done, n + 1)
                if n >= 2:
                    ve.wait_ge(pt_done, key_blocks(n - 1))
                mask = K[:, C_PREV:C_PREV + w] if nk == 2 else (
                    K[:, C_BLOCK:C_BLOCK + P] if g == 2 else K[:, C_CAUSAL:C_CAUSAL + P])
                src = ps[:, 4:6, :].rearrange("p e (q w) -> p e q w", q=2)[:, :, :, 0:w]
                dst = S1[:, n % 2, :, :, 0:w]
                ve.tensor_tensor(dst, src, mask.unsqueeze(1).unsqueeze(1).broadcast_to([P, 2, 2, w]), ALU.add
                                 ).then_inc(s_read, 1)
                ve.wait_ge(s_read, n + 1)
                link(ve.tensor_reduce(md[:, n, 0, :].rearrange("p (e q) -> p e q", e=2), dst, X, ALU.max))
                ve.tensor_scalar(negm[:, n, :], md[:, n, 0, :], -DH ** -0.5, None, ALU.mult).then_inc(negm_ready, 1)

            def back(n):
                g, b, _ = TILES1[n]
                ve.wait_ge(pv_done, n + 1)
                src = ps[:, 7, 0:2 * P].rearrange("p (q t) -> p q t", q=2)
                st = ps[0:GH, 7, 2 * P:4 * P].rearrange("p (q t) -> p q t", q=2)
                o = oT[:, 2 * g:2 * g + 2, :]
                s = stats[:, :, g, :]
                if g == 0:
                    o, s = o[:, :, b * P:(b + 1) * P], s[:, :, b * P:(b + 1) * P]
                else:
                    o = o.rearrange("p c (i r) -> p c r i", r=TT)[:, :, b, :]
                    s = s.rearrange("p c (i r) -> p c r i", r=TT)[:, :, b, :]
                ve.tensor_copy(o, src).then_inc(pv_read, 1)
                ve.tensor_copy(s, st).then_inc(pv_read, 1)

            def combine():
                ve.wait_ge(pv_read, 2 * len(TILES1))
                link(ve.tensor_tensor(amax[:, 0, :], stats[:, 0, 0, :], stats[:, 0, 1, :], ALU.max))
                link(ve.tensor_tensor(amax[:, 0, :], amax[:, 0, :], stats[:, 0, 2, :], ALU.max))
                wide = [GH, GROUPS, S]
                ve.tensor_tensor(alpha[:], stats[:, 0, :, :], amax[:, 0, :].unsqueeze(1).broadcast_to(wide), ALU.subtract
                                 ).then_inc(gap_ready, 1)
                ve.wait_ge(gap_exp, 1)
                link(ve.tensor_tensor(stats[:, 1, :, :], stats[:, 1, :, :], alpha[:], ALU.mult))
                link(ve.tensor_tensor(amax[:, 0, :], stats[:, 1, 0, :], stats[:, 1, 1, :], ALU.add))
                link(ve.tensor_tensor(amax[:, 0, :], amax[:, 0, :], stats[:, 1, 2, :], ALU.add))
                link(ve.reciprocal(amax[:, 1, :], amax[:, 0, :]))
                ve.tensor_tensor(alpha[:], alpha[:], amax[:, 1, :].unsqueeze(1).broadcast_to(wide), ALU.mult
                                 ).then_inc(alpha_ready, 1)
                for hp in range(2):
                    ve.wait_ge(alpha_spread, hp + 1)
                    if hp:
                        ve.wait_ge(cat_lo, 3)
                    for g in range(GROUPS):
                        ins = ve.tensor_tensor(comb[:, g, :], oT[:, 2 * g + hp, :], ps[:, 4 * (1 - hp) + g, :], ALU.mult)
                    link(ins)
                    link(ve.tensor_tensor(comb[:, 0, :], comb[:, 0, :], comb[:, 1, :], ALU.add))
                    ve.tensor_tensor(comb[:, 0, :], comb[:, 0, :], comb[:, 2, :], ALU.add).then_inc(attn_ready, 1)
                    ve.wait_ge(attn_ready, hp + 1)
                    ve.wait_ge(cat_hi, 3 + hp)
                    ve.tensor_tensor(hL[:, 2 + hp, :], comb[:, 0, :], hH[:, 2 + hp, :].bitcast(F32), ALU.subtract
                                     ).then_inc(cat_lo, 1)

            def up(f):
                d0 = (D_UP1, D_UP2)[f]
                done = 2 * FF_PAIRS * f
                own0 = own[0]
                per = 2 + 2 * f
                with ve.Fori(0, FF_PAIRS) as j:
                    n = [0]

                    def conv(m, half):
                        t, z = act[:, 2 * half + m, :], ps[:, 2 * half + m, :]
                        if f == 0:
                            w1, w0 = v("conv_w", j * 2 + (22 + m)), v("conv_w", j * 2 + m)
                            ve.wait_ge(seeded, j * 2 + (m + 1))
                        else:
                            w1, w0 = v("ffn_conv_w_2", j * 2 + (44 + 22 * half + m)), v("ffn_conv_w_2", j * 2 + (22 * half + m))
                            ve.wait_ge(seeded, j * 4 + (2 * FF_PAIRS + 2 * half + m + 1))
                        n[0] += 1
                        ve.scalar_tensor_tensor(out=t[:, 1:S], in0=z[:, 0:S - 1], scalar=w1, in1=t[:, 1:S],
                                                op0=ALU.mult, op1=ALU.add).then_inc(dve_own, 1)
                        ve.wait_ge(dve_own, j * per + (own0 + n[0]))
                        return ve.scalar_tensor_tensor(out=t[:, 2:S], in0=z[:, 0:S - 2], scalar=w0, in1=t[:, 2:S],
                                                       op0=ALU.mult, op1=ALU.add)

                    conv(0, 0).then_inc(gate_conv, 1)
                    conv(1, 0).then_inc(gate_conv, 1)
                    if f == 1:
                        conv(0, 1).then_inc(val_conv, 1)
                        conv(1, 1).then_inc(val_conv, 1)
                        ve.wait_ge(val_conv, j * 2 + 4)
                    for m in range(2):
                        ve.wait_ge(gelu_done, j * 2 + (m + 1 + done))
                        if f == 0:
                            ve.wait_ge(pe_seg, j * 4 + 2 * d0 + 3 + m)
                            other = ps[:, 2 + m, :]
                        else:
                            other = act[:, 2 + m, :]
                        ve.tensor_tensor(act[:, m, :], act[:, m, :], other, ALU.mult).then_inc(hid_ready, 1)
                    for m in range(2):
                        ve.wait_ge(hid_hi, j * 2 + (m + 1 + done))
                        ve.tensor_tensor(hidL[:, bass.ds(j * 2 + m, 1), :], act[:, m:m + 1, :],
                                         hidH[:, bass.ds(j * 2 + m, 1), :].bitcast(F32), ALU.subtract).then_inc(hid_lo, 1)
                    assert n[0] == per
                own[0] += per * FF_PAIRS

            def bias_rows():
                ve.wait_ge(rel_done, 1)
                ve.tensor_tensor(rrow[:, 0:S], ps[0:HEADS2, 6, :], hot[0:HEADS2, REL:REL + S], ALU.add).then_inc(rrow_ready, 1)
                ve.tensor_tensor(rrow[:, S:REL], ps[0:HEADS2, 7, 0:P], hot[0:HEADS2, REL + S:2 * REL], ALU.add
                                 ).then_inc(rrow_ready, 1)

            def evac_in2(d):
                r = d - D_IN2
                kind, j = r // 2, r % 2
                if kind == 0 and j == 0:
                    for k in (KD - 2, KD - 1):
                        wait_h(ve, N_PRE2, k)
                    ve.memset(cc[:, :, 0:2], 0.0).then_inc(pads_zero, 1)
                elif kind == 1:
                    ve.wait_ge(pe_seg, 2 * d + 2)
                    ve.wait_ge(banks_read[j], bank_use(d - 2) + 1)
                    t = cc[:, 2 * j:2 * j + 2, 2:]
                    ve.tensor_tensor(t, t, banks(d), ALU.mult).then_inc(banks_read[j], 1)
                elif kind == 2:
                    ve.wait_ge(banks_read[j], bank_use(d))
                    ve.wait_ge(pads_zero, 2)
                    for m in range(2):
                        c = 2 * j + m
                        link(ve.tensor_scalar(nt[:, m, :], cc[:, c, 2:2 + S], v("conv_mix_w_2", 8 + c), None, ALU.mult))
                        for tap in (1, 0):
                            link(ve.scalar_tensor_tensor(out=nt[:, m, :], in0=cc[:, c, tap:tap + S],
                                                         scalar=v("conv_mix_w_2", 4 * tap + c), in1=nt[:, m, :],
                                                         op0=ALU.mult, op1=ALU.add))
                    ve.wait_ge(pe_seg, 2 * d + 2)
                    for m in range(2):
                        c = 2 * j + m
                        if j == 1:
                            ve.wait_ge(conv_lo, c - 1)
                        ve.tensor_tensor(sq[:, m, :], nt[:, m, :], ps[:, 2 * pair_of(d) + m, :], ALU.mult
                                         ).then_inc(banks_read[j] if m else conv_y, 1)
                    for m in range(2):
                        c = 2 * j + m
                        ve.wait_ge(conv_hi, c + 1)
                        ve.tensor_tensor(bufAL[:, c, :], sq[:, m, :], bufAH[:, c, :].bitcast(F32), ALU.subtract
                                         ).then_inc(conv_lo, 1)

            def evac_br(d):
                br = next(i for i, d0 in ((2, D_BR2), (1, D_BR1), (0, D_BR0)) if d >= d0)
                j, r = (d - (D_BR0, D_BR1, D_BR2)[br]) // 2, (d - D_BR0) % 2
                if not r:
                    return
                g = d - 1
                ve.wait_ge(banks_read[pair_of(g)], bank_use(g) + 1)
                for m in range(2):
                    c = 2 * j + m
                    ve.wait_ge(pe_seg, 2 * d + 1 + m)
                    z = ps[:, 2 * pair_of(d) + m, :]
                    ins = ve.tensor_tensor(sg[:, m, :], sg[:, m, :], z, ALU.mult)
                    if m == 0:
                        link(ins)
                    else:
                        ins.then_inc(banks_read[pair_of(d)], 1)
                        ve.wait_ge(banks_read[pair_of(d)], bank_use(d) + 1)
                    if br == 0:
                        ve.wait_ge(rrow_stored, 16)
                        ve.tensor_copy(merged[:, c, :], sg[:, m, :]).then_inc(merged_ready, 1)
                    else:
                        ve.tensor_tensor(merged[:, c, :], merged[:, c, :], sg[:, m, :], ALU.add).then_inc(merged_ready, 1)

            def front2(n):
                kind, i, h, nb, _, _ = tile2(n)
                w = P * nb
                ve.wait_ge(s2_done, n + 1)
                if n >= 2:
                    ve.wait_ge(pt2_done, n - 1)
                if kind == "self":
                    if n == 0:
                        ve.wait_ge(bias_loaded, 32)
                    bias = (W0 if h < 4 else W1)[:, h % 4, S - w:S]
                    ve.scalar_tensor_tensor(out=S2[:, n % 2, 0:w], in0=ps[:, 4 + n % 2, 0:w], scalar=DH ** -0.5, in1=bias,
                                            op0=ALU.mult, op1=ALU.add).then_inc(s2_read, 1)
                    ve.wait_ge(s2_read, n + 1)
                    ve.tensor_reduce(md2[:, 0, n:n + 1], S2[:, n % 2, 0:w], X, ALU.max, negate=True).then_inc(negm2_ready, 1)
                else:
                    link(ve.tensor_reduce(md2[:, 2, n:n + 1], ps[:, 4 + n % 2, 0:w], X, ALU.max))
                    ve.tensor_scalar(md2[:, 0, n:n + 1], md2[:, 2, n:n + 1], -P ** -0.5, None, ALU.mult
                                     ).then_inc(negm2_ready, 1)

            def mid2(n):
                w = P * tile2(n)[3]
                ve.wait_ge(exp2_done, n + 1)
                link(ve.reciprocal(md2[:, 2, n:n + 1], md2[:, 1, n:n + 1]))
                ve.tensor_scalar(S2[:, n % 2, 0:w], S2[:, n % 2, 0:w], md2[:, 2, n:n + 1], None, ALU.mult
                                 ).then_inc(p2_scaled, 1)

            def lo2(n):
                kind, i, h, _, c, row = tile2(n)
                if kind == "self" and row == 0:
                    return
                hi, lo = (bufBH, bufBL) if kind == "self" else (bufAH, bufAL)
                q = slice(i * P, (i + 1) * P)
                ve.wait_ge(o2_hi, pairs_before(n) + 1)
                ve.tensor_tensor(lo[:, c, q], ps[:, 7, 0:P], hi[:, c, q].bitcast(F32), ALU.subtract).then_inc(o2_lo, 1)

            def merge(c):
                ve.wait_ge(m_hi, c + 1)
                ve.tensor_tensor(mgL[:, c, :], merged[:, c, :], mgH[:, c, :].bitcast(F32), ALU.subtract).then_inc(m_lo, 1)

            def finish():
                for t in range(TT):
                    ve.wait_ge(out_turned, t + 1)
                    src = ps[:, 2 * (t % 2):2 * (t % 2) + 2, :]
                    ve.tensor_copy(otok[:, t, :].rearrange("p (b n) -> p b n", b=2), src).then_inc(out_copied, 1)

            walk({"start": start, "ada": ada, "ada_end": ada_end, "norm": norm, "apply": apply, "resid": resid, "evac_in": evac_in,
                  "turn": turn, "pool": pool_step, "front": front, "back": back, "combine": combine, "up": up,
                  "bias_rows": bias_rows, "evac_in2": evac_in2, "evac_br": evac_br, "front2": front2, "mid2": mid2,
                  "lo2": lo2, "merge": merge, "finish": finish})

        @block.tensor
        def _(pe):
            def start():
                pe.wait_ge(k_loaded, 16)
                pe.wait_ge(vec_loaded, 16 * len(VEC))
                for t, r in enumerate(TABLE_ROWS):
                    mm = pe.transpose(ps[:, 4, t * P:t * P + r], vrow[0:r, t, :], ident_t[0:r, 0:r])
                mm.then_inc(vec_turned, 1)
                pe.wait_ge(x_loaded, 16 * TT)
                for k in range(KD):
                    if k >= 3:
                        pe.wait_ge(x_ready, k - 2)
                    for t in range(TT):
                        mm = pe.transpose(ps[:, k % 3, t * P:(t + 1) * P], xtok[:, t, k * P:(k + 1) * P], ident)
                    mm.then_inc(x_turned, 1)

            def ada_turn(n):
                for used in ada_summed:
                    pe.wait_ge(used, n + 1)
                bank = 3 if n < ADA_FIRST else 7
                for m in range(2):
                    for x in range(2):
                        mm = pe.matmul(ps[:, bank, 2 * n + m:2 * n + m + 1], acc[:, n % 2, x, m * P:(m + 1) * P],
                                       ones[:, 0:1], start=(x == 0), stop=(x == 1))
                mm.then_inc(ada_turned, 1)

            def squares(n, k):
                w = norm_source[n][1]
                if n == 0 and k == 0:
                    pe.wait_ge(ones_ready, 1)
                if k == 0 and n:
                    pe.wait_ge(var_ready, n)
                pe.wait_ge(sq_ready, KD * n + k + 1)
                pe.matmul(ps[:, 5, 0:w], ones[:], sq[:, k % 2, 0:w], start=(k == 0), stop=(k == KD - 1)
                          ).then_inc(ss_added, 1)

            def norm(n):
                pe.wait_ge(diag_ready, n + 1)
                for t in range(norm_source[n][1] // P):
                    mm = pe.matmul(ps[:, 4, t * P:(t + 1) * P], ones[:], nt[:, 1, t * P:(t + 1) * P], start=True, stop=True)
                mm.then_inc(rstd_ready, 1)

            def product(out, lhs, rhs, first, last):
                for i, (x, y) in enumerate(((0, 0), (0, 1), (1, 0))):
                    mm = pe.matmul(out, lhs[x], rhs[y], start=(first and i == 0), stop=(last and i == 2))
                return mm

            def source_of(d):
                if D_DOWN1 <= d < D_IN2 or d >= D_DOWN2:
                    return hidH, hidL
                for d0, buf in ((D_BR0, (bufAH, bufAL)), (D_BR1, (bufBH, bufBL)), (D_BR2, (bufAH, bufAL))):
                    if d0 <= d < d0 + 8 and (d - d0) % 2:
                        return buf
                if D_KV <= d < D_KV + 4:
                    return memH, memL
                if D_OUT2 <= d < D_UP2:
                    return mgH, mgL
                return hH, hL

            first_of = {D_IN: N_PRE1, D_IN2: N_PRE2, D_KV: N_MEM}

            def seg(d, m, k_from=0, k_to=None):
                p = pair_of(d)
                down = D_DOWN1 <= d < D_IN2 or d >= D_DOWN2
                q = ((d - D_DOWN1) % 4 if d < D_IN2 else (d - D_DOWN2) % 4) if down else 0
                if m == 0 and k_from == 0:
                    pe.wait_ge(lo_done, d + 1)
                    if q == 0 and bank_use(d) > 0:
                        pe.wait_ge(banks_read[p], bank_use(d))
                    if d == D_OUT:
                        pe.wait_ge(cat_lo, 4)
                    if d in (D_DOWN1, D_DOWN2):
                        pe.wait_ge(hid_lo, 2 + (1 if d == D_DOWN1 else 2) * 2 * FF_PAIRS)
                    if d == D_BR0 + 1:
                        pe.wait_ge(conv_lo, 4)
                    if d == D_BR1 + 1:
                        pe.wait_ge(o2_lo, pairs_before(len(TILES2)))
                    if d == D_BR2 + 1:
                        pe.wait_ge(o2_lo, pairs_before(len(TILES23)))
                    if d == D_OUT2:
                        pe.wait_ge(m_lo, KD)
                src = source_of(d)
                _, nk = unit_source(d)
                k0 = DOWN_K0[q] if down else 0
                s = d % 2
                by_token = (D_IN < d < D_OUT) or (D_IN2 + 10 <= d < D_BR0) or d in (D_KV + 2, D_KV + 3)
                if not by_token:
                    w = MEM if D_KV <= d < D_KV + 4 else S
                    if d in first_of and m == 1:
                        return
                    for k in range(k_from, nk if k_to is None else k_to):
                        if d in first_of:
                            wait_h(pe, first_of[d], k)
                        for half in (0, 1) if d in first_of else (m,):
                            cols = slice(half * P, (half + 1) * P)
                            mm = product(ps[:, 2 * p + half, 0:w], (WH[:, s, k, cols], WL[:, s, k, cols]),
                                         (src[0][:, k0 + k, :], src[1][:, k0 + k, :]),
                                         k == 0 and q == 0, k == nk - 1 and (not down or q == 3))
                            if d in first_of and k == nk - 1 and half == 0:
                                mm.then_inc(pe_seg, 1)
                else:
                    g = (d - 1) // 3 if d < D_OUT else 0
                    tiles = (m,) if d >= D_KV else (2 * m, 2 * m + 1)
                    for t in tiles:
                        o = ps[:, 2 * p + m, t % 2 * UC:t % 2 * UC + UC] if d < D_KV else ps[:, 2 * p + m, 0:UC]
                        for k in range(nk):
                            mm = product(o, (tokens(src[0], k, g, t), tokens(src[1], k, g, t)),
                                         (WH[:, s, k, :], WL[:, s, k, :]), k == 0, k == nk - 1)
                if k_to is None or k_to == nk:
                    mm.then_inc(pe_seg, 1)

            def turn(e):
                pe.wait_ge(rope_done, 2 * e + 2)
                for hp in range(2):
                    if e:
                        pe.wait_ge(turn_read, 2 * (e - 1) + hp + 1)
                    for t in range(TT):
                        mm = pe.transpose(ps[:, 5 + hp, t * P:(t + 1) * P], qtok[:, e % 2, t, hp * P:(hp + 1) * P], ident)
                    mm.then_inc(turned, 1)

            def pool_step():
                pe.wait_ge(wpool_loaded, 16)
                pe.wait_ge(banks_read[0], 5)
                pe.wait_ge(banks_read[1], 5)
                pe.wait_ge(pool_mixed, 8)
                for m in range(2):
                    for half in range(2):
                        r = slice(64 * half, 64 * half + 64)
                        mm = pe.matmul(ps[r, 2 * m + half, :], wpool[r, m, :], u[r, m, POOL_PAD:], start=True, stop=True)
                    mm.then_inc(pool_done, 1)

            def front(n):
                g, b, nk = TILES1[n]
                pe.wait_ge(turn_read, 12)
                if n:
                    pe.wait_ge(s_read, n)
                k0 = P * (b - 1) if nk == 2 else P * b
                for q in range(2):
                    for e in range(2):
                        r = slice(64 * e, 64 * e + 64)
                        mm = pe.matmul(ps[:, 4 + e, 256 * q:256 * q + P * nk], qT[r, 2 * g + q, P * b:P * b + P],
                                       kT[r, 2 * g + q, k0:k0 + P * nk], start=True, stop=True)
                mm.then_inc(s_done, 1)

            def mid(n):
                pe.wait_ge(exp_done, GH * (n + 1))
                for kb in range(TILES1[n][2]):
                    i = key_blocks(n) + kb
                    if i:
                        pe.wait_ge(pt_read, i)
                    for x in range(GH):
                        mm = pe.transpose(ps[:, 6, P * x:P * x + P],
                                          S1[:, n % 2, x // 2, x % 2, P * kb:P * kb + P], ident)
                    mm.then_inc(pt_done, 1)

            def back(n):
                g, b, nk = TILES1[n]
                pe.wait_ge(pt_read, key_blocks(n + 1))
                if n:
                    pe.wait_ge(pv_read, 2 * n)
                else:
                    pe.wait_ge(mod_ready, 4)
                pe.wait_ge(banks_read[pair_of(3 + 3 * g)], bank_use(3 + 3 * g) + 1)
                for q in range(2):
                    for e in range(2):
                        h = 2 * q + e
                        for kb in range(nk):
                            pe.matmul(ps[64 * e:64 * e + 64, 7, P * q:P * q + P],
                                      V1[:, b - nk + 1 + kb, g, DH * h:DH * h + DH],
                                      PT1[:, n % 2, kb, P * (2 * e + q):P * (2 * e + q) + P],
                                      start=(kb == 0), stop=(kb == nk - 1))
                for i in range(2):
                    mm = pe.transpose(ps[0:GH, 7, P * (2 + i):P * (3 + i)], md[:, n, i, :], ident)
                mm.then_inc(pv_done, 1)

            def combine():
                pe.wait_ge(alpha_ready, 1)
                pe.wait_ge(pool_val, 4)
                for hp in range(2):
                    for g in range(GROUPS):
                        mm = pe.matmul(ps[:, 4 * (1 - hp) + g, :], K[0:GH, C_SEL + P * hp:C_SEL + P * hp + P],
                                       alpha[:, g, :], start=True, stop=True)
                    mm.then_inc(alpha_spread, 1)

            def up(f):
                d0 = (D_UP1, D_UP2)[f]
                done = 2 * FF_PAIRS * f
                first = (N_PREF1, N_PREF2)[f]
                pe.wait_ge(banks_read[0], bank_use(d0))
                pe.wait_ge(banks_read[1], bank_use(d0))
                with pe.Fori(0, FF_PAIRS) as j:
                    for half in range(2):
                        pe.wait_ge(lo_done, j * 2 + (d0 + half + 1))
                        if half == 0:
                            pe.wait_ge(gate_conv, j * 2 + (2 + done))
                        elif f == 0:
                            pe.wait_ge(hid_ready, j * 2 + 2)
                        else:
                            pe.wait_ge(val_conv, j * 2 + 2)
                        def tile(k, m):
                            cols = slice(m * P, (m + 1) * P)
                            mm = product(ps[:, 2 * half + m, :], (WH[:, half, k, cols], WL[:, half, k, cols]),
                                         (hH[:, k, :], hL[:, k, :]), k == 0, k == KD - 1)
                            if k == KD - 1:
                                mm.then_inc(pe_seg, 1)

                        if half == 0:
                            for k in range(KD):
                                wait_h(pe, first, k)
                                tile(k, 0)
                                tile(k, 1)
                        else:
                            for m in range(2):
                                for k in range(KD):
                                    tile(k, m)

            def bias_rows():
                pe.wait_ge(hot_loaded, 32)
                pe.matmul(ps[0:HEADS2, 6, :], rel[:], hot[:, 0:S], start=True, stop=True)
                pe.matmul(ps[0:HEADS2, 7, 0:P], rel[:], hot[:, S:REL], start=True, stop=True).then_inc(rel_done, 1)

            def front2(n):
                kind, i, h, nb, c, row = tile2(n)
                if n >= 2:
                    pe.wait_ge(exp2_done, n - 1)
                qs = slice(i * P, (i + 1) * P)
                if kind == "self":
                    if n == 0:
                        pe.wait_ge(banks_read[0], bank_use(D_BR0))
                        pe.wait_ge(banks_read[1], bank_use(D_BR0 + 1))
                    r = slice(row, row + DH)
                    mm = pe.matmul(ps[:, 4 + n % 2, 0:P * nb], q2[r, c, qs], k2[r, c, 0:P * nb], start=True, stop=True)
                else:
                    if n == len(TILES2):
                        pe.wait_ge(banks_read[0], bank_use(D_BR1))
                        pe.wait_ge(banks_read[1], bank_use(D_BR1 + 1))
                    mm = pe.matmul(ps[:, 4 + n % 2, 0:MEM], qm[:, c, qs], mk[:, c, :], start=True, stop=True)
                mm.then_inc(s2_done, 1)

            def mid2(n):
                nb = tile2(n)[3]
                pe.wait_ge(p2_scaled, n + 1)
                if n:
                    pe.wait_ge(pt2_read, n)
                for b in range(nb):
                    mm = pe.transpose(ps[:, 6, P * b:P * b + P], S2[:, n % 2, P * b:P * b + P], ident)
                mm.then_inc(pt2_done, 1)

            def back2(n):
                kind, i, h, nb, c, row = tile2(n)
                pe.wait_ge(pt2_read, n + 1)
                if pairs_before(n):
                    pe.wait_ge(o2_lo, pairs_before(n))
                for b in range(nb):
                    if kind == "self":
                        out, val = ps[row:row + DH, 7, 0:P], V2[:, b, DH * h:DH * h + DH]
                    else:
                        out, val = ps[:, 7, 0:P], mv[:, b, P * h:P * h + P]
                    mm = pe.matmul(out, val, PT2[:, n % 2, P * b:P * b + P], start=(b == 0), stop=(b == nb - 1))
                mm.then_inc(pv2_done, 1)

            def mem_turn():
                pe.wait_ge(mem_loaded, 16 * (MEM // P))
                pe.wait_ge(o2_lo, pairs_before(len(TILES2)))
                for k in range(KD):
                    if k >= 2:
                        pe.wait_ge(mem_ready, k - 1)
                    for t in range(MEM // P):
                        mm = pe.transpose(ps[:, 6 + k % 2, t * P:(t + 1) * P], memtok[:, t, k * P:(k + 1) * P], ident)
                    mm.then_inc(mem_turned, 1)

            def finish():
                for t in range(TT):
                    if t >= 2:
                        pe.wait_ge(out_copied, t - 1)
                    for k in (KD - 1, KD - 2, KD - 3):
                        wait_x(pe, N_POSTF2, k)
                    for k in range(KD):
                        mm = pe.transpose(ps[:, 2 * (t % 2) + k // 4, k % 4 * P:(k % 4 + 1) * P],
                                          xT[:, k, t * P:(t + 1) * P], ident)
                    mm.then_inc(out_turned, 1)

            walk({"start": start, "ada_turn": ada_turn, "squares": squares, "norm": norm, "seg": seg, "turn": turn, "pool": pool_step, "front": front,
                  "mid": mid, "back": back, "combine": combine, "up": up, "bias_rows": bias_rows, "front2": front2,
                  "mid2": mid2, "back2": back2, "mem_turn": mem_turn, "finish": finish})


def tables():
    import numpy as np

    t = np.zeros((P, C_END), np.float32)
    t[:, C_ID:C_ID + P] = np.eye(P)
    q, kk = np.arange(P)[:, None], np.arange(P)[None, :]
    k = t[:, P:]
    k[:, C_PREV:C_PREV + P] = np.where(kk >= q, 0.0, NEG)
    k[:, C_CAUSAL:C_CAUSAL + P] = np.where(kk <= q, 0.0, NEG)
    k[:, C_BLOCK:C_BLOCK + P] = np.where((kk <= q) & (kk % 4 == q % 4), 0.0, NEG)
    k[:, C_FREQ:C_FREQ + 8] = np.float32(500000.0) ** (-np.arange(0, 16, 2, dtype=np.float32) / np.float32(16))
    for x in range(GH):
        e, c = x // 2, x % 2
        k[x, C_SEL + P * c + 64 * e:C_SEL + P * c + 64 * e + 64] = 1.0
    for g, w in enumerate(WINDOWS):
        r = slice(64 * (g % 2), 64 * (g % 2) + 64)
        k[r, C_RC + 16 * (g // 2):C_RC + 16 * (g // 2) + 16] = 1.0 / np.minimum(np.arange(16) + 1.0, w)
        k[r, C_RW + g // 2] = 1.0 / w
    hot = np.zeros((BUCKETS, 2 * REL), np.float32)
    dist = np.arange(S)
    far = np.maximum(dist, BUCKETS // 2).astype(np.float32)
    large = BUCKETS // 2 + (np.log(far / np.float32(16)) / np.float32(np.log(64.0)) * np.float32(16)).astype(np.int32)
    bucket = np.where(dist < BUCKETS // 2, dist, np.minimum(large, BUCKETS - 1))
    hot[bucket[::-1], np.arange(S)] = 1.0
    hot[:, REL + S:] = NEG
    return t, hot


_ROWS = {"c": 8, "b_ada": 48, "g_pre_mix": 8, "g_post_mix": 8, "g_pre_ffn": 8, "g_post_ffn": 8, "b_pool": 2,
         "pool_scale": 2, "b_gate_2": 24, "conv_w": 66, "conv_b": 22, "g_pre_mix_2": 8, "g_post_mix_2": 8,
         "g_pre_ffn_2": 8, "g_post_ffn_2": 8, "g_mem_2": 8, "ffn_conv_w_2": 132, "conv_mix_w_2": 12,
         "ffn_conv_b_2": 44}
_SHAPES = {"x": (S, D), "positions": (S,), "w_ada": (D, 6 * D), "w_in": (D, 2560), "w_pool": (4, DH, DH),
           "w_out": (512, D), "w_up": (D, 2 * D_FF), "w_down": (D_FF, D), "mem_2": (MEM, D),
           "rel_bias_2": (BUCKETS, HEADS2), "w_in_2": (D, 6656), "w_conv_out_2": (512, D),
           "w_attn_out_2": (512, D), "w_mem_kv_2": (D, D), "w_mem_out_2": (512, D), "w_out_2": (D, D),
           "w_up_2": (D, 2 * D_FF), "w_down_2": (D_FF, D)}


def kernel(**inputs):
    import numpy as np
    import concourse.bacc as bacc
    from concourse.bass_utils import run_bass_kernel_spmd

    nc = bacc.Bacc("TRN2", target_bir_lowering=False, num_devices=1)
    arrays, aps = {}, {}
    shapes = dict(_SHAPES, **{n: (r, P) for n, r in _ROWS.items()})
    table, hot = tables()
    given = {n: np.ascontiguousarray(inputs[n]).reshape(shape) for n, shape in shapes.items()}
    given.update(table=table, hot=hot)
    pos = given["positions"]
    given["positions"] = np.concatenate([pos.reshape(TT, P).T, pos.reshape(P, TT), pos.reshape(P, TT)], axis=1)
    for name, x in given.items():
        arrays[name + "_dram"] = x
        aps[name] = nc.dram_tensor(name + "_dram", x.shape, mybir.dt.from_np(x.dtype), kind="ExternalInput").ap()
    out = nc.dram_tensor("out_dram", (S, D), F32, kind="ExternalOutput").ap()
    build(nc, aps, out)
    r = run_bass_kernel_spmd(nc, [arrays], core_ids=[0])
    return r.results[0]["out_dram"].reshape(1, S, D)
```
